# Optimizing a Trainium2 kernel written in Bass

```python
import jax, jax.numpy as jnp
from jax import lax
import numpy as np

D_MODEL = 1024
BATCH = 1
SEQ = 256
DEPTH = 2

HEAD_DIM = 64
ROT_DIM = HEAD_DIM // 4
ROPE_THETA = 500000.0
ATTN_SCALE = HEAD_DIM ** -0.5
EPS = 1e-6
NEG_INF = -1e30

MOBA_HEADS = 8
FOX_HEADS = 8
MOBA_BLOCK = 256
MOBA_TOPK = 3
MOBA_Q_CHUNK = 64
FOX_Q_BLOCK = 128
A_W = MOBA_HEADS * HEAD_DIM
B_W = FOX_HEADS * HEAD_DIM
EVEN_COLS = 3 * A_W + 4 * B_W + FOX_HEADS
EVEN_MIX_WIDTH = A_W + B_W

SWA_Q_HEADS = 16
SWA_KV_HEADS = 2
SWA_WINDOW = 128
ODD_COLS = (SWA_Q_HEADS + 2 * SWA_KV_HEADS) * HEAD_DIM
ODD_MIX_WIDTH = SWA_Q_HEADS * HEAD_DIM

PEER_HEADS = 8
PEER_N_KEYS = 128
PEER_N_EXPERTS = PEER_N_KEYS * PEER_N_KEYS
PEER_TOPK = 16
PEER_QUERY_DIM = 128
PEER_TOKEN_CHUNK = 128

N_EVEN = (DEPTH + 1) // 2
N_ODD = DEPTH // 2

kernel_name = "hybrid_moba_fox_swa_peer"

def rms_norm(x, g):
    x32 = x.astype(jnp.float32)
    y = x32 * lax.rsqrt(jnp.mean(x32 * x32, axis=-1, keepdims=True) + EPS)
    return y.astype(x.dtype) * g

def rope_tables(seq):
    inv_freq = jnp.power(ROPE_THETA, -jnp.arange(0, ROT_DIM, 2, dtype=jnp.float32) / ROT_DIM)
    ang = jnp.arange(seq, dtype=jnp.float32)[:, None] * inv_freq[None, :]
    return jnp.cos(ang), jnp.sin(ang)

def partial_rope(x, cos, sin):
    x32 = x.astype(jnp.float32)
    half = ROT_DIM // 2
    x1 = x32[..., :half]
    x2 = x32[..., half:ROT_DIM]
    out = jnp.concatenate([x1 * cos - x2 * sin, x2 * cos + x1 * sin, x32[..., ROT_DIM:]], axis=-1)
    return out.astype(x.dtype)

def split_heads(t, n):
    b, s, _ = t.shape
    return t.reshape(b, s, n, HEAD_DIM).transpose(0, 2, 1, 3)

def merge_heads(t):
    b, h, s, d = t.shape
    return t.transpose(0, 2, 1, 3).reshape(b, s, h * d)

def moba_attention(q, k, v):
    B, H, S, D = q.shape
    Sp = -(-S // MOBA_BLOCK) * MOBA_BLOCK
    pad = ((0, 0), (0, 0), (0, Sp - S), (0, 0))
    q, k, v = jnp.pad(q, pad), jnp.pad(k, pad), jnp.pad(v, pad)
    nb = Sp // MOBA_BLOCK
    topk = min(MOBA_TOPK, nb)
    kb = k.reshape(B, H, nb, MOBA_BLOCK, D)
    vb = v.reshape(B, H, nb, MOBA_BLOCK, D)
    kmean = jnp.mean(kb.astype(jnp.float32), axis=3).astype(k.dtype)
    bi = jnp.arange(B)[:, None, None, None]
    hi = jnp.arange(H)[None, :, None, None]
    blk_ids = jnp.arange(nb)

    def step(c):
        start = c * MOBA_Q_CHUNK
        blk = start // MOBA_BLOCK
        qc = lax.dynamic_slice_in_dim(q, start, MOBA_Q_CHUNK, axis=2)
        gate = jnp.einsum('bhqd,bhnd->bhqn', qc, kmean).astype(jnp.float32)
        gate = jnp.where(blk_ids < blk, gate, -jnp.inf)
        _, sel = lax.top_k(gate, topk)
        valid = sel < blk
        ks = kb[bi, hi, sel]
        vs = vb[bi, hi, sel]
        ls = jnp.einsum('bhqd,bhqnkd->bhqnk', qc, ks).astype(jnp.float32) * ATTN_SCALE
        ls = jnp.where(valid[..., None], ls, NEG_INF)
        kown = lax.dynamic_index_in_dim(kb, blk, axis=2, keepdims=False)
        vown = lax.dynamic_index_in_dim(vb, blk, axis=2, keepdims=False)
        lo = jnp.einsum('bhqd,bhkd->bhqk', qc, kown).astype(jnp.float32) * ATTN_SCALE
        qpos = start + jnp.arange(MOBA_Q_CHUNK)
        kpos = blk * MOBA_BLOCK + jnp.arange(MOBA_BLOCK)
        lo = jnp.where(kpos[None, :] <= qpos[:, None], lo, NEG_INF)
        logits = jnp.concatenate([ls.reshape(B, H, MOBA_Q_CHUNK, topk * MOBA_BLOCK), lo], axis=-1)
        p = jax.nn.softmax(logits, axis=-1).astype(v.dtype)
        ps = p[..., :topk * MOBA_BLOCK].reshape(B, H, MOBA_Q_CHUNK, topk, MOBA_BLOCK)
        po = p[..., topk * MOBA_BLOCK:]
        return (jnp.einsum('bhqnk,bhqnkd->bhqd', ps, vs)
                + jnp.einsum('bhqk,bhkd->bhqd', po, vown))

    out = lax.map(step, jnp.arange(Sp // MOBA_Q_CHUNK))
    out = out.transpose(1, 2, 0, 3, 4).reshape(B, H, Sp, D)
    return out[:, :, :S]

def fox_attention(q, k, v, log_F):
    B, H, S, D = q.shape
    kpos = jnp.arange(S)

    def step(i):
        start = i * FOX_Q_BLOCK
        qb = lax.dynamic_slice_in_dim(q, start, FOX_Q_BLOCK, axis=2)
        fq = lax.dynamic_slice_in_dim(log_F, start, FOX_Q_BLOCK, axis=2)
        logits = (jnp.einsum('bhqd,bhkd->bhqk', qb, k).astype(jnp.float32) * ATTN_SCALE
                  + fq[..., :, None] - log_F[:, :, None, :])
        qpos = start + jnp.arange(FOX_Q_BLOCK)
        logits = jnp.where(kpos[None, :] <= qpos[:, None], logits, NEG_INF)
        p = jax.nn.softmax(logits, axis=-1).astype(v.dtype)
        return jnp.einsum('bhqk,bhkd->bhqd', p, v)

    out = lax.map(step, jnp.arange(S // FOX_Q_BLOCK))
    return out.transpose(1, 2, 0, 3, 4).reshape(B, H, S, D)

def sliding_window_attention(q, k, v, sinks):
    B, Hq, S, D = q.shape
    Hkv = k.shape[1]
    G = Hq // Hkv
    W = SWA_WINDOW
    nb = S // W
    qb = q.reshape(B, Hkv, G, nb, W, D)

    def band(t):
        tb = t.reshape(B, Hkv, nb, W, D)
        prev = jnp.concatenate([jnp.zeros_like(tb[:, :, :1]), tb[:, :, :-1]], axis=2)
        return jnp.concatenate([prev, tb], axis=3)

    kc, vc = band(k), band(v)
    logits = jnp.einsum('bkgnqd,bknjd->bkgnqj', qb, kc).astype(jnp.float32) * ATTN_SCALE
    i = jnp.arange(W)[:, None]
    j = jnp.arange(2 * W)[None, :]
    n = jnp.arange(nb)[:, None, None]
    dist = W + i - j
    allowed = (dist >= 0) & (dist < SWA_WINDOW) & (n * W + j - W >= 0)
    logits = jnp.where(allowed, logits, NEG_INF)
    sink = jnp.broadcast_to(sinks.astype(jnp.float32).reshape(1, Hkv, G, 1, 1, 1),
                            logits.shape[:-1] + (1,))
    p = jax.nn.softmax(jnp.concatenate([logits, sink], axis=-1), axis=-1)[..., :2 * W]
    o = jnp.einsum('bkgnqj,bknjd->bkgnqd', p.astype(v.dtype), vc)
    return o.reshape(B, Hq, S, D)

def even_mixer(h, w_in, f_bias, qn_a, kn_a, qn_b, kn_b, w_out, cos, sin):
    proj = h @ w_in
    offs = [A_W, 2 * A_W, 3 * A_W, 3 * A_W + B_W, 3 * A_W + 2 * B_W, 3 * A_W + 3 * B_W, 3 * A_W + 4 * B_W]
    qa, ka, va, qb, kb, vb, gb, fb = jnp.split(proj, offs, axis=-1)
    qa = partial_rope(rms_norm(split_heads(qa, MOBA_HEADS), qn_a), cos, sin)
    ka = partial_rope(rms_norm(split_heads(ka, MOBA_HEADS), kn_a), cos, sin)
    oa = moba_attention(qa, ka, split_heads(va, MOBA_HEADS))
    qb = rms_norm(split_heads(qb, FOX_HEADS), qn_b)
    kb = rms_norm(split_heads(kb, FOX_HEADS), kn_b)
    log_f = jax.nn.log_sigmoid((fb + f_bias).astype(jnp.float32)).transpose(0, 2, 1)
    log_F = jnp.cumsum(log_f, axis=-1)
    ob = fox_attention(qb, kb, split_heads(vb, FOX_HEADS), log_F)
    ob = merge_heads(ob) * jax.nn.sigmoid(gb)
    return jnp.concatenate([merge_heads(oa), ob], axis=-1) @ w_out

def odd_mixer(h, w_in, qn, kn, sinks, w_out, cos, sin):
    proj = h @ w_in
    qw = SWA_Q_HEADS * HEAD_DIM
    kw = SWA_KV_HEADS * HEAD_DIM
    q, k, v = jnp.split(proj, [qw, qw + kw], axis=-1)
    q = partial_rope(rms_norm(split_heads(q, SWA_Q_HEADS), qn), cos, sin)
    k = partial_rope(rms_norm(split_heads(k, SWA_KV_HEADS), kn), cos, sin)
    o = sliding_window_attention(q, k, split_heads(v, SWA_KV_HEADS), sinks)
    return merge_heads(o) @ w_out

def peer_ffn(h, w_query, sub_keys, expert_down, expert_up):
    B, S, D = h.shape
    T = B * S
    ht = h.reshape(T, D)
    q = (ht @ w_query).reshape(T, PEER_HEADS, 2, PEER_QUERY_DIM // 2)
    s = jnp.einsum('thpd,hpnd->thpn', q, sub_keys).astype(jnp.float32)
    s1, i1 = lax.top_k(s[:, :, 0], PEER_TOPK)
    s2, i2 = lax.top_k(s[:, :, 1], PEER_TOPK)
    cand = (s1[..., :, None] + s2[..., None, :]).reshape(T, PEER_HEADS, PEER_TOPK * PEER_TOPK)
    cand_idx = (i1[..., :, None] * PEER_N_KEYS + i2[..., None, :]).reshape(T, PEER_HEADS, PEER_TOPK * PEER_TOPK)
    top_s, pos = lax.top_k(cand, PEER_TOPK)
    idx = jnp.take_along_axis(cand_idx, pos, axis=-1)
    g = jax.nn.softmax(top_s, axis=-1)
    nc = T // PEER_TOKEN_CHUNK

    def chunk(args):
        xc, ic, gc = args
        u = expert_down[ic]
        a = jax.nn.gelu(jnp.einsum('cd,chkd->chk', xc, u).astype(jnp.float32), approximate=False)
        w = (gc * a).astype(xc.dtype)
        return jnp.einsum('chk,chkd->cd', w, expert_up[ic])

    out = lax.map(chunk, (ht.reshape(nc, PEER_TOKEN_CHUNK, D),
                          idx.reshape(nc, PEER_TOKEN_CHUNK, PEER_HEADS, PEER_TOPK),
                          g.reshape(nc, PEER_TOKEN_CHUNK, PEER_HEADS, PEER_TOPK)))
    return out.reshape(B, S, D)

def setup_inputs(seed: int = 0) -> dict:
    key = jax.random.key(seed)
    ks = jax.random.split(key, 20)
    f32 = jnp.float32

    def nrm(k, shape, scale):
        return jax.random.normal(k, shape, f32) * scale

    def gain(k, shape):
        return 1.0 + 0.05 * jax.random.normal(k, shape, f32)

    return {
        "x": jax.random.normal(ks[0], (BATCH, SEQ, D_MODEL), f32),
        "attn_norm": gain(ks[1], (DEPTH, D_MODEL)),
        "ffn_norm": gain(ks[2], (DEPTH, D_MODEL)),
        "ev_w_in": nrm(ks[3], (N_EVEN, D_MODEL, EVEN_COLS), D_MODEL ** -0.5),
        "ev_forget_bias": 2.0 + 0.1 * jax.random.normal(ks[4], (N_EVEN, FOX_HEADS), f32),
        "ev_q_norm_a": gain(ks[5], (N_EVEN, HEAD_DIM)),
        "ev_k_norm_a": gain(ks[6], (N_EVEN, HEAD_DIM)),
        "ev_q_norm_b": gain(ks[7], (N_EVEN, HEAD_DIM)),
        "ev_k_norm_b": gain(ks[8], (N_EVEN, HEAD_DIM)),
        "ev_w_out": nrm(ks[9], (N_EVEN, EVEN_MIX_WIDTH, D_MODEL), EVEN_MIX_WIDTH ** -0.5),
        "od_w_in": nrm(ks[10], (N_ODD, D_MODEL, ODD_COLS), D_MODEL ** -0.5),
        "od_q_norm": gain(ks[11], (N_ODD, HEAD_DIM)),
        "od_k_norm": gain(ks[12], (N_ODD, HEAD_DIM)),
        "od_sinks": nrm(ks[13], (N_ODD, SWA_Q_HEADS), 0.5),
        "od_w_out": nrm(ks[14], (N_ODD, ODD_MIX_WIDTH, D_MODEL), ODD_MIX_WIDTH ** -0.5),
        "peer_w_query": nrm(ks[15], (DEPTH, D_MODEL, PEER_HEADS * PEER_QUERY_DIM), D_MODEL ** -0.5),
        "peer_sub_keys": nrm(ks[16], (DEPTH, PEER_HEADS, 2, PEER_N_KEYS, PEER_QUERY_DIM // 2),
                             (PEER_QUERY_DIM // 2) ** -0.5),
        "peer_down": nrm(ks[17], (DEPTH, PEER_N_EXPERTS, D_MODEL), D_MODEL ** -0.5),
        "peer_up": nrm(ks[18], (DEPTH, PEER_N_EXPERTS, D_MODEL), 0.25),
    }

def reference(x, attn_norm, ffn_norm, ev_w_in, ev_forget_bias, ev_q_norm_a, ev_k_norm_a,
              ev_q_norm_b, ev_k_norm_b, ev_w_out, od_w_in, od_q_norm, od_k_norm, od_sinks,
              od_w_out, peer_w_query, peer_sub_keys, peer_down, peer_up):
    S = x.shape[1]
    cos, sin = rope_tables(S)
    for l in range(DEPTH):
        h = rms_norm(x, attn_norm[l])
        i = l // 2
        if l % 2 == 0:
            x = x + even_mixer(h, ev_w_in[i], ev_forget_bias[i], ev_q_norm_a[i], ev_k_norm_a[i],
                               ev_q_norm_b[i], ev_k_norm_b[i], ev_w_out[i], cos, sin)
        else:
            x = x + odd_mixer(h, od_w_in[i], od_q_norm[i], od_k_norm[i], od_sinks[i],
                              od_w_out[i], cos, sin)
        h = rms_norm(x, ffn_norm[l])
        x = x + peer_ffn(h, peer_w_query[l], peer_sub_keys[l], peer_down[l], peer_up[l])
    return x


_drawn_inputs = setup_inputs


def setup_inputs(seed=0):
    import zlib

    import numpy as np

    out = dict(_drawn_inputs(seed))
    spreads = {}
    factors = {'ev_q_norm_a': 2.922,
     'ev_k_norm_a': 2.998,
     'ev_q_norm_b': 3.061,
     'ev_k_norm_b': 3.222,
     'od_q_norm': 4.161,
     'od_k_norm': 4.321,
     'od_sinks': 32.042}
    for name, (base, spread) in spreads.items():
        noise = np.random.default_rng([zlib.crc32(name.encode()), seed]).standard_normal(out[name].shape)
        drawn = base * np.exp(spread * noise) if base else spread * noise
        out[name] = __import__('jax').numpy.asarray(drawn.astype(out[name].dtype))
    for name, factor in factors.items():
        out[name] = (out[name] * factor).astype(out[name].dtype)
    return out
```

```python
from contextlib import ExitStack

import concourse.bass as bass
from concourse import mybir

ALU = mybir.AluOpType
ACT = mybir.ActivationFunctionType
F32 = mybir.dt.float32
BF16 = mybir.dt.bfloat16
U32 = mybir.dt.uint32
AX_X = mybir.AxisListType.X

P = 128
D = 1024
KT = D // P
HD = 64
HEADS = 16
EPS = 1e-6
NEG_INF = -1e30
BIG = 3.0e38
SCALE = HD ** -0.5
ROT = 8
CW = 512
PH = 8
TK = 16
NK = 128
EXPERTS = NK * NK
STAGES = [(0, 0), (0, 1), (1, 0), (1, 1)]
RING = 8
DIAGS = 4
WSLOTS = 2
AUGW = HD + 2

C_ID, C_M0, C_TRI, C_ONES, C_M1, C_COS, C_SIN, C_IOTA, C_EPS, C_END = 0, 128, 384, 512, 640, 896, 912, 928, 944, 945

CHUNKS = [[(CW * c, CW) for c in range(7)] + [(7 * CW, 8)], [(0, CW), (CW, CW), (2 * CW, 256)]]
SPLITS = [(0, 2), (2, 4), (4, 6), (6, 7)]


def q_head(layer, j):
    return j if layer == 1 or j < 8 else 16 + j - 8


def k_head(layer, j):
    return 16 + j // 8 if layer == 1 else 8 + j if j < 8 else 24 + j - 8


def k_rows(layer, j):
    return HD if layer == 1 or j < 8 else AUGW


class Banks:

    def __init__(self, full, free, tensors, uses):
        self.full, self.free, self.tensors = full, free, tensors
        self.number = {u: n for n, u in enumerate(uses)}

    def bank(self, use):
        return self.tensors[self.number[use] % 2]

    def freed(self, use):
        return self.free[self.number[use] % 2]

    def wait_room(self, eng, use):
        n = self.number[use]
        if n >= 2:
            eng.wait_ge(self.free[n % 2], n // 2)

    def wait_full(self, eng, use):
        eng.wait_ge(self.full, self.number[use] + 1)

    def wait_evacuated(self, eng, use):
        n = self.number[use]
        eng.wait_ge(self.free[n % 2], n // 2 + 1)


def build(nc, x_in, consts, attn_norm, ffn_norm, w_in0, fbias, head_gains0, w_out0, w_in1,
          head_gains1, sinks, w_out1, w_query, keys_t, down, up, out):
    ctx = ExitStack()
    with ctx:
        def sb(name, shape, dt=F32):
            return ctx.enter_context(nc.sbuf_tensor(name, shape, dt))

        def sem(name):
            return ctx.enter_context(nc.semaphore(name))

        cst = sb("cst", [P, C_END])
        ident = cst[:, C_ID:C_ID + P]
        masks = [cst[:, C_M0:C_M0 + 2 * P], cst[:, C_M1:C_M1 + 2 * P]]
        tri = cst[:, C_TRI:C_TRI + P]
        ones = cst[:, C_ONES:C_ONES + P]
        iota = cst[:, C_IOTA:C_IOTA + TK]
        eps = cst[:, C_EPS:C_EPS + 1]
        down_rows = sb("down_rows", [P, RING, D])
        up_rows = sb("up_rows", [P, RING, D])
        diags = sb("diags", [P, DIAGS, P])
        x = sb("x", [P, 2, D])
        h_ffn = sb("h_ffn", [P, 2, D])
        gain_attn = sb("gain_attn", [P, D])
        gain_ffn = sb("gain_ffn", [P, D])
        act_t = sb("act_t", [P, KT, P])
        weights = sb("weights", [P, WSLOTS, KT, CW])
        keys = sb("keys", [HD, 2 * PH, NK])
        raw = sb("raw", [P, 4 * CW])
        h_attn = raw[:, 0:D]
        attended = raw[:, 0:D]
        queries = raw[:, D:2 * D]
        aug = sb("aug", [P, 32, AUGW])
        onehot = aug[:, :, :].rearrange("p a b -> p (a b)")[:, 0:PH * TK * TK]
        q_t = sb("q_t", [AUGW, HEADS, P])
        k_t = sb("k_t", [AUGW, HEADS, 2 * P])
        v = sb("v", [P, 2, D])
        gate = sb("gate", [P, CW])
        probs = sb("probs", [P, 2, 2 * P])
        probs_t = sb("probs_t", [P, 2, 2 * P])
        ids = sb("ids", [P, 4 * PH * TK], U32)
        gates = sb("gates", [P, 4 * PH * TK])
        down_ids = sb("down_ids", [P, TK], U32)
        up_ids = sb("up_ids", [P, TK], U32)
        dots = sb("dots", [P, TK])
        gelus = sb("gelus", [P, TK])
        w_next = sb("w_next", [P, TK])
        w_now = sb("w_now", [P, TK])
        g_heads = [sb("g_heads0", [P, 4, HD]), sb("g_heads1", [P, 2, HD])]
        sink = sb("sink", [P, HEADS])
        f_bias = sb("f_bias", [P, 8])
        sumsq = sb("sumsq", [P, 1])
        rms = sb("rms", [P, 1])
        rstd = sb("rstd", [P, 1])
        head_ss = sb("head_ss", [P, 32])
        rope_tmp = raw[:, 0:4 * 18 * ROT].rearrange("p (a h r) -> p a h r", a=4, h=18)
        fz = sb("fz", [P, 4, 8])
        log_f = sb("log_f", [P, 2, 8])
        neg_max = sb("neg_max", [P, HEADS])
        row_sum = sb("row_sum", [P, HEADS])
        sink_e = sb("sink_e", [P, HEADS])
        neg_sink = sb("neg_sink", [P, HEADS])
        top_v = sb("top_v", [P, 2 * PH, TK])
        top_i = sb("top_i", [P, 2 * PH, TK], U32)
        rest = sb("rest", [P, TK * TK])
        cand = sb("cand", [P, TK * TK])
        best_v = sb("best_v", [P, PH, TK])
        best_i = sb("best_i", [P, PH, TK], U32)
        top_if = raw[:, 0:2 * PH * TK].rearrange("p (a b) -> p a b", a=2 * PH)
        half_i = raw[:, 256:384].bitcast(U32)
        half_f = raw[:, 384:512]
        id_1 = raw[:, 512:640]
        id_2 = raw[:, 640:768]
        g_sum = sb("g_sum", [P, PH])

        def bank(name):
            return ctx.enter_context(nc.psum_tensor(name, [P, CW], F32))

        acc = [bank("acc0"), bank("acc1")]
        mm_banks = [bank("mm0"), bank("mm1")]
        tp_banks = [bank("tp0"), bank("tp1")]
        o_banks = [bank("o0"), bank("o1")]

        consts_in = sem("consts_in")
        x_in_sem = [sem("x_in0"), sem("x_in1")]
        norms_in = sem("norms_in")
        keys_in = sem("keys_in")
        weights_in = [sem(f"weights_in{i}") for i in range(WSLOTS)]
        mm_full, mm_free = sem("mm_full"), [sem("mm_free0"), sem("mm_free1")]
        tp_full, tp_free = sem("tp_full"), [sem("tp_free0"), sem("tp_free1")]
        dve_step = sem("dve_step")
        ss1_ready, rms1_ready, h1_ready = sem("ss1_ready"), sem("rms1_ready"), sem("h1_ready")
        rms2_ready, head_ss_ready, head_rms_ready = sem("rms2_ready"), sem("head_ss_ready"), sem("head_rms_ready")
        squares_ready, aug_ready = sem("squares_ready"), sem("aug_ready")
        fz_ready, fe_ready, fln_ready = sem("fz_ready"), sem("fe_ready"), sem("fln_ready")
        log_f_ready, f_ready = sem("log_f_ready"), sem("f_ready")
        probs_ready = sem("probs_ready")
        pv_done, o_free = sem("pv_done"), sem("o_free")
        sink_in_ready, sink_e_ready = sem("sink_in_ready"), sem("sink_e_ready")
        gated = sem("gated")
        ss2_ready, h2_ready = sem("ss2_ready"), sem("h2_ready")
        best_ready, gexp_ready, ids_ready = sem("best_ready"), sem("gexp_ready"), sem("ids_ready")
        down_in = [sem(f"down_in{i}") for i in range(RING)]
        up_in = [sem(f"up_in{i}") for i in range(RING)]
        down_staged, up_staged = sem("down_staged"), sem("up_staged")
        slots_claimed = sem("slots_claimed")
        dots_done, gelu_done = sem("dots_done"), sem("gelu_done")
        w_ready, w_taken = sem("w_ready"), sem("w_taken")
        diag_ready, up_done = sem("diag_ready"), sem("up_done")
        x_out_ready, out_written = sem("x_out_ready"), sem("out_written")

        mm_uses, tp_uses, chunk_list = [], [], []
        for s, (l, t) in enumerate(STAGES):
            n = len(CHUNKS[l])
            mm_uses += [("proj", s, c) for c in range(n)] + [("F", s)] * (l == 0)
            mm_uses += [("S", s, j) for j in range(HEADS)] + [("out", s, c) for c in range(2)]
            mm_uses += [("wq", s, c) for c in range(2)] + [("sc", s, g) for g in range(4)]
            tp_uses += [("h1", s, i) for i in range(2)] + [("qk", s, g) for g in range(8 if l == 0 else 5)]
            tp_uses += [("PT", s, j) for j in range(HEADS)] + [("att", s, i) for i in range(2)]
            tp_uses += [("h2", s, i) for i in range(2)] + [("pq", s, g) for g in range(4)]
            chunk_list += [("proj", s, c) for c in range(n)] + [("out", s, c) for c in range(2)]
            chunk_list += [("wq", s, c) for c in range(2)]
        mm = Banks(mm_full, mm_free, mm_banks, mm_uses)
        tp = Banks(tp_full, tp_free, tp_banks, tp_uses)
        chunk_no = {c: n for n, c in enumerate(chunk_list)}

        def chunk_cols(use):
            kind, s, c = use
            return CHUNKS[STAGES[s][0]][c] if kind == "proj" else (CW * c, CW)

        def chunk_source(use):
            kind, s, c = use
            l = STAGES[s][0]
            a, w = chunk_cols(use)
            m = {"proj": (w_in0, w_in1), "out": (w_out0, w_out1), "wq": (w_query[0], w_query[1])}[kind][l]
            return m[:, a:a + w].rearrange("(kt p) n -> p kt n", p=P)

        def qk_group(s, g):
            l = STAGES[s][0]
            if g < 4:
                return [(q_head(l, j), j, k_rows(l, j)) for j in range(4 * g, 4 * g + 4)]
            if l == 0:
                return [(k_head(l, j), j, k_rows(l, j)) for j in range(4 * (g - 4), 4 * (g - 4) + 4)]
            return [(16 + i, i, HD) for i in range(2)]

        def v_cols(l, j):
            return slice(HD * j, HD * j + HD) if l == 0 else slice(HD * (j // 8), HD * (j // 8) + HD)

        def wait_residual(eng, s):
            for c in range(2):
                mm.wait_evacuated(eng, ("out", s, c))

        block = ctx.enter_context(nc.Block())

        @block.sync
        def _(sp):
            sp.dma_start(x[:, 0, :], x_in[0:P, :]).then_inc(x_in_sem[0], 16)
            sp.dma_start(cst[:, :], consts).then_inc(consts_in, 16)

            def layer_gains(l):
                sp.dma_start(gain_attn[:, :], attn_norm[l].partition_broadcast(P)).then_inc(norms_in, 16)
                sp.dma_start(gain_ffn[:, :], ffn_norm[l].partition_broadcast(P)).then_inc(norms_in, 16)
                sp.dma_start(keys[:, :, :], keys_t[:, l]).then_inc(keys_in, 16)

            layer_gains(0)
            sp.dma_start(g_heads[0][:, :, :], head_gains0.partition_broadcast(P)).then_inc(consts_in, 16)
            sp.dma_start(g_heads[1][:, :, :], head_gains1.partition_broadcast(P)).then_inc(consts_in, 16)
            sp.dma_start(sink[:, :], sinks.partition_broadcast(P)).then_inc(consts_in, 16)
            sp.dma_start(f_bias[:, :], fbias.partition_broadcast(P)).then_inc(consts_in, 16)
            for n, use in enumerate(chunk_list):
                if use == ("proj", 2, 0):
                    sp.wait_ge(h2_ready, 2)
                    mm.wait_full(sp, ("sc", 1, 3))
                    layer_gains(1)
                if n >= WSLOTS:
                    mm.wait_full(sp, chunk_list[n - WSLOTS])
                w = chunk_cols(use)[1]
                sp.dma_start(weights[:, n % WSLOTS, :, 0:w], chunk_source(use)).then_inc(weights_in[n % WSLOTS], 16)
                if n == 1:
                    sp.dma_start(x[:, 1, :], x_in[P:2 * P, :]).then_inc(x_in_sem[1], 16)
            for t in range(2):
                sp.wait_ge(x_out_ready, 2 * (2 + t) + 2)
                sp.dma_start(out[t * P:(t + 1) * P, :], x[:, t, :]).then_inc(out_written, 16)
            sp.wait_ge(out_written, 32)

        @block.gpsimd
        def _(pool):
            def gather(table, rows, ids_now, k, landed):
                pool.sem_inc(slots_claimed, 1)
                pool.indirect_dma_start(
                    out=rows[:, k % RING, :], out_offset=None, in_=table,
                    in_offset=bass.IndirectOffsetOnAxis(ap=ids_now[:, k:k + 1], axis=0)).then_inc(landed[k % RING], 16)

            def group(g, with_down=True, with_up=True):
                first = isinstance(g, int) and g < 0
                if with_down and isinstance(g, int) and (g + 1) % PH == 0:
                    pool.wait_ge(ids_ready, (g + 1) // PH + 1)
                for half in range(TK // RING):
                    a = half * RING
                    for k in range(a, a + RING):
                        if with_down:
                            if not first:
                                pool.wait_ge(dots_done, TK * (g + 1) + k + 1 - RING)
                            elif k >= RING:
                                pool.wait_ge(dots_done, k + 1 - RING)
                            if k == a:
                                nc.gpsimd.tensor_copy(down_ids[:, a:a + RING],
                                                      ids[:, bass.ds(TK * (g + 1) + a, RING)]).then_inc(down_staged, 1)
                                pool.wait_ge(down_staged, 2 * g + 3 + half)
                            gather(down, down_rows, down_ids, k, down_in)
                        if with_up:
                            if not (isinstance(g, int) and TK * g + k + 1 - RING <= 0):
                                pool.wait_ge(up_done, TK * g + k + 1 - RING)
                            if k == a:
                                nc.gpsimd.tensor_copy(up_ids[:, a:a + RING],
                                                      ids[:, bass.ds(TK * g + a, RING)]).then_inc(up_staged, 1)
                                pool.wait_ge(up_staged, 2 * g + 1 + half)
                            gather(up, up_rows, up_ids, k, up_in)

            group(-1, with_up=False)
            for s in range(4):
                for a, b in SPLITS:
                    if s == 0 and a == 0:
                        group(0)
                        a = 1
                    if b - a > 1:
                        with pool.Fori(PH * s + a, PH * s + b) as g:
                            group(g)
                    else:
                        group(PH * s + a)
                group(PH * s + PH - 1, with_down=s < 3)

        @block.scalar
        def _(act):
            def evacuate(banks, use, dst, src):
                banks.wait_full(act, use)
                nc.scalar.copy(dst, src).then_inc(banks.freed(use), 1)

            def transposed(kind, s):
                for i in range(2):
                    evacuate(tp, (kind, s, i), act_t[:, 4 * i:4 * i + 4, :],
                             tp.bank((kind, s, i))[:, :].rearrange("p (a b) -> p a b", a=4))

            def front(s, piece):
                l, t = STAGES[s]
                nkeys = (t + 1) * P
                if piece == 0:
                    if l == 0:
                        act.wait_ge(x_in_sem[t], 16)
                    else:
                        act.wait_ge(x_out_ready, 2 * (s - 2) + 2)
                    if s:
                        act.wait_ge(ids_ready, s)
                    nc.scalar.activation(h_attn, x[:, t, :], ACT.Square, accum_out=sumsq[:, :]).then_inc(ss1_ready, 1)
                    act.wait_ge(ss1_ready, s + 1)
                    nc.scalar.activation(rms[:, :], sumsq[:, :], ACT.Sqrt, scale=1.0 / D, bias=eps).then_inc(rms1_ready, 1)
                    if s:
                        mm.wait_full(act, ("wq", s - 1, 1))
                    transposed("h1", s)
                    for c, (a, w) in enumerate(CHUNKS[l]):
                        use = ("proj", s, c)
                        b = mm.bank(use)
                        if l == 0:
                            if c in (0, 1, 3, 4):
                                i = (0, 1, None, 2, 3)[c]
                                evacuate(mm, use, raw[:, CW * i:CW * i + CW], b[:, :])
                            elif c in (2, 5):
                                i = c // 5
                                evacuate(mm, use, v[:, t, CW * i:CW * i + CW], b[:, :])
                            elif c == 6:
                                mm.wait_full(act, use)
                                nc.scalar.activation(gate[:, :], b[:, :], ACT.Exp, scale=-1.0).then_inc(mm.freed(use), 1)
                        elif c < 2:
                            evacuate(mm, use, raw[:, CW * c:CW * c + CW], b[:, :])
                        else:
                            mm.wait_full(act, use)
                            nc.scalar.copy(raw[:, 2 * CW:2 * CW + P], b[:, 0:P])
                            nc.scalar.copy(v[:, t, 0:P], b[:, P:2 * P]).then_inc(mm.freed(use), 1)
                    nh = 32 if l == 0 else 18
                    for c in range(len(CHUNKS[l]) - (1 if l == 0 else 0)):
                        mm.wait_evacuated(act, ("proj", s, c))
                    nc.scalar.activation(aug[:, 0:nh, 0:HD], raw[:, 0:nh * HD].rearrange("p (h d) -> p h d", d=HD),
                                         ACT.Square).then_inc(squares_ready, 1)
                    act.wait_ge(head_ss_ready, s + 1)
                    nc.scalar.activation(head_ss[:, 0:nh], head_ss[:, 0:nh], ACT.Sqrt, scale=1.0 / HD,
                                         bias=eps).then_inc(head_rms_ready, 1)
                    if l == 0:
                        act.wait_ge(fz_ready, s + 1)
                        nc.scalar.activation(fz[:, 2, :], fz[:, 1, :], ACT.Exp).then_inc(fe_ready, 1)
                        act.wait_ge(fe_ready, s + 1)
                        nc.scalar.activation(fz[:, 3, :], fz[:, 2, :], ACT.Ln, bias=1.0).then_inc(fln_ready, 1)
                    for g in range(8 if l == 0 else 5):
                        heads = qk_group(s, g)
                        use = ("qk", s, g)
                        n, rows = len(heads), heads[0][2]
                        j = heads[0][1]
                        src = tp.bank(use)[0:rows, 0:n * P].rearrange("p (a b) -> p a b", a=n)
                        dst = q_t[0:rows, j:j + n, :] if g < 4 else k_t[0:rows, j:j + n, t * P:(t + 1) * P]
                        evacuate(tp, use, dst, src)
                elif piece == 1:
                    def transposed_probs(j):
                        if j >= 2 or s:
                            act.wait_ge(pv_done, HEADS * s + j - 1)
                        evacuate(tp, ("PT", s, j), probs_t[:, j % 2, 0:nkeys], tp.bank(("PT", s, j))[:, 0:nkeys])

                    for j in range(HEADS):
                        mm.wait_evacuated(act, ("S", s, j))
                        nc.scalar.activation(probs[:, j % 2, 0:nkeys], probs[:, j % 2, 0:nkeys], ACT.Exp,
                                             scale=-1.0, bias=neg_max[:, j:j + 1],
                                             accum_out=row_sum[:, j:j + 1]).then_inc(probs_ready, 1)
                        if j:
                            transposed_probs(j - 1)
                        if l == 1 and j % 8 == 7:
                            i = j // 8
                            act.wait_ge(sink_in_ready, 2 * t + i + 1)
                            nc.scalar.activation(sink_e[:, 8 * i:8 * i + 8], sink_e[:, 8 * i:8 * i + 8],
                                                 ACT.Exp).then_inc(sink_e_ready, 1)
                    transposed_probs(HEADS - 1)
                    mm.wait_full(act, ("proj", s, len(CHUNKS[l]) - 1))
                    transposed("att", s)
                else:
                    wait_residual(act, s)
                    nc.scalar.activation(queries, x[:, t, :], ACT.Square, accum_out=sumsq[:, :]).then_inc(ss2_ready, 1)
                    act.wait_ge(ss2_ready, s + 1)
                    nc.scalar.activation(rms[:, :], sumsq[:, :], ACT.Sqrt, scale=1.0 / D, bias=eps).then_inc(rms2_ready, 1)
                    mm.wait_full(act, ("out", s, 1))
                    transposed("h2", s)
                    for c in range(2):
                        evacuate(mm, ("wq", s, c), queries[:, CW * c:CW * c + CW], mm.bank(("wq", s, c))[:, :])
                    for g in range(4):
                        evacuate(tp, ("pq", s, g), q_t[0:HD, 4 * g:4 * g + 4, :],
                                 tp.bank(("pq", s, g))[0:HD, :].rearrange("p (a b) -> p a b", a=4))
                    act.wait_ge(best_ready, s + 1)
                    nc.scalar.activation(best_v[:, :, :], best_v[:, :, :], ACT.Exp).then_inc(gexp_ready, 1)

            def gelu(g):
                act.wait_ge(dots_done, TK * (g + 1))
                nc.scalar.activation(gelus[:, :], dots[:, :], ACT.Gelu).then_inc(gelu_done, 1)

            def group(g, with_down=True):
                act.wait_ge(w_ready, g + 1)
                nc.scalar.copy(w_now[:, :], w_next[:, :]).then_inc(w_taken, 1)
                act.wait_ge(w_taken, g + 1)
                for k in range(TK):
                    if not (isinstance(g, int) and TK * g + k + 1 - DIAGS <= 0):
                        act.wait_ge(up_done, TK * g + k + 1 - DIAGS)
                    nc.scalar.activation(diags[:, k % DIAGS, :], ident, ACT.Copy,
                                         scale=w_now[:, k:k + 1]).then_inc(diag_ready, 1)
                if with_down:
                    gelu(g + 1)

            act.wait_ge(consts_in, 5 * 16)
            for piece in range(3):
                front(0, piece)
            gelu(0)
            for s in range(4):
                for i, (a, b) in enumerate(SPLITS):
                    if s == 0 and a == 0:
                        group(0)
                        a = 1
                    if b - a > 1:
                        with act.Fori(PH * s + a, PH * s + b) as g:
                            group(g)
                    else:
                        group(PH * s + a)
                    if s < 3 and i < 3:
                        front(s + 1, i)
                group(PH * s + PH - 1, with_down=s < 3)
                act.wait_ge(up_done, PH * TK * (s + 1))
                for c in range(2):
                    nc.scalar.copy(x[:, STAGES[s][1], CW * c:CW * c + CW], acc[c][:, :]).then_inc(x_out_ready, 1)

        @block.tensor
        def _(pe):
            def transposes(kind, s, src):
                for i in range(2):
                    use = (kind, s, i)
                    tp.wait_room(pe, use)
                    for k in range(4):
                        last = nc.tensor.transpose(tp.bank(use)[:, k * P:(k + 1) * P],
                                                   src[:, (4 * i + k) * P:(4 * i + k + 1) * P], ident)
                    last.then_inc(tp_full, 1)

            def project(use):
                n = chunk_no[use]
                w = chunk_cols(use)[1]
                pe.wait_ge(weights_in[n % WSLOTS], 16 * (n // WSLOTS + 1))
                mm.wait_room(pe, use)
                for k in range(KT):
                    last = nc.tensor.matmul(mm.bank(use)[:, 0:w], act_t[:, k, :], weights[:, n % WSLOTS, k, 0:w],
                                            start=(k == 0), stop=(k == KT - 1))
                last.then_inc(mm_full, 1)

            def front(s, piece):
                l, t = STAGES[s]
                nkeys = (t + 1) * P
                if piece == 0:
                    pe.wait_ge(h1_ready, s + 1)
                    transposes("h1", s, h_attn)
                    for i in range(2):
                        tp.wait_evacuated(pe, ("h1", s, i))
                    for c in range(len(CHUNKS[l])):
                        project(("proj", s, c))
                    if l == 0:
                        use = ("F", s)
                        pe.wait_ge(log_f_ready, s + 1)
                        mm.wait_room(pe, use)
                        if t:
                            nc.tensor.matmul(mm.bank(use)[:, 0:8], ones, log_f[:, 0, :], start=True, stop=False)
                        nc.tensor.matmul(mm.bank(use)[:, 0:8], tri, log_f[:, t, :], start=(t == 0),
                                         stop=True).then_inc(mm_full, 1)
                    pe.wait_ge(aug_ready, s + 1)
                    for g in range(8 if l == 0 else 5):
                        use = ("qk", s, g)
                        tp.wait_room(pe, use)
                        for i, (place, _, rows) in enumerate(qk_group(s, g)):
                            last = nc.tensor.transpose(tp.bank(use)[0:rows, i * P:(i + 1) * P], aug[:, place, 0:rows], ident)
                        last.then_inc(tp_full, 1)
                elif piece == 1:
                    for g in range(8 if l == 0 else 5):
                        tp.wait_evacuated(pe, ("qk", s, g))

                    def scores(j):
                        use = ("S", s, j)
                        rows = k_rows(l, j)
                        mm.wait_room(pe, use)
                        kj = j if l == 0 else j // 8
                        nc.tensor.matmul(mm.bank(use)[:, 0:nkeys], q_t[0:rows, j, :], k_t[0:rows, kj, 0:nkeys],
                                         start=True, stop=True).then_inc(mm_full, 1)

                    def values(j):
                        use = ("PT", s, j)
                        tp.wait_evacuated(pe, use)
                        if j % 8 == 0 and s:
                            pe.wait_ge(o_free, 2 * (s - 1) + j // 8 + 1)
                        o = o_banks[j // 8][:, (j % 8) * HD:(j % 8 + 1) * HD]
                        for i in range(t + 1):
                            last = nc.tensor.matmul(o, probs_t[:, j % 2, i * P:(i + 1) * P], v[:, i, v_cols(l, j)],
                                                    start=(i == 0), stop=(i == t))
                        last.then_inc(pv_done, 1)

                    scores(0)
                    scores(1)
                    for j in range(HEADS):
                        use = ("PT", s, j)
                        tp.wait_room(pe, use)
                        pe.wait_ge(probs_ready, HEADS * s + j + 1)
                        for i in range(t + 1):
                            last = nc.tensor.transpose(tp.bank(use)[:, i * P:(i + 1) * P],
                                                       probs[:, j % 2, i * P:(i + 1) * P], ident)
                        last.then_inc(tp_full, 1)
                        if j + 2 < HEADS:
                            scores(j + 2)
                        if j:
                            values(j - 1)
                    values(HEADS - 1)
                    pe.wait_ge(o_free, 2 * s + 2)
                    if l == 0:
                        pe.wait_ge(gated, s + 1)
                    transposes("att", s, attended)
                    for i in range(2):
                        tp.wait_evacuated(pe, ("att", s, i))
                    for c in range(2):
                        project(("out", s, c))
                else:
                    pe.wait_ge(h2_ready, s + 1)
                    transposes("h2", s, h_ffn[:, s % 2, :])
                    for i in range(2):
                        tp.wait_evacuated(pe, ("h2", s, i))
                    for c in range(2):
                        project(("wq", s, c))
                    for c in range(2):
                        mm.wait_evacuated(pe, ("wq", s, c))
                    for g in range(4):
                        use = ("pq", s, g)
                        tp.wait_room(pe, use)
                        for i in range(4):
                            last = nc.tensor.transpose(tp.bank(use)[0:HD, i * P:(i + 1) * P],
                                                       queries[:, (4 * g + i) * HD:(4 * g + i + 1) * HD], ident)
                        last.then_inc(tp_full, 1)
                    pe.wait_ge(keys_in, 16 * (l + 1))
                    for g in range(4):
                        use = ("sc", s, g)
                        tp.wait_evacuated(pe, ("pq", s, g))
                        mm.wait_room(pe, use)
                        for i in range(4):
                            last = nc.tensor.matmul(mm.bank(use)[:, i * NK:(i + 1) * NK], q_t[0:HD, 4 * g + i, :],
                                                    keys[:, 4 * g + i, :], start=True, stop=True)
                        last.then_inc(mm_full, 1)

            def residual(s):
                wait_residual(pe, s)
                if s:
                    pe.wait_ge(x_out_ready, 2 * s)
                for c in range(2):
                    nc.tensor.matmul(acc[c][:, :], ident, x[:, STAGES[s][1], CW * c:CW * c + CW], start=True, stop=False,
                                     skip_group_check=True)

            def group(g, last=False):
                for k in range(TK):
                    pe.wait_ge(diag_ready, TK * g + k + 1)
                    pe.wait_ge(up_in[k % RING], 16 * (TK // RING * g + k // RING + 1))
                    for c in range(2):
                        ins = nc.tensor.matmul(acc[c][:, :], diags[:, k % DIAGS, :], up_rows[:, k % RING, CW * c:CW * c + CW],
                                               start=False, stop=(last and k == TK - 1), skip_group_check=True)
                    ins.then_inc(up_done, 1)

            pe.wait_ge(consts_in, 5 * 16)
            for piece in range(3):
                front(0, piece)
            for s in range(4):
                residual(s)
                for i, (a, b) in enumerate(SPLITS):
                    if b - a > 1:
                        with pe.Fori(PH * s + a, PH * s + b) as g:
                            group(g)
                    else:
                        group(PH * s + a)
                    if s < 3 and i < 3:
                        front(s + 1, i)
                group(PH * s + PH - 1, last=True)

        @block.vector
        def _(dve):
            steps = [0]

            def tick(ins):
                steps[0] += 1
                return ins.then_inc(dve_step, 1)

            def settle():
                dve.wait_ge(dve_step, steps[0])

            def link(ins):
                tick(ins)
                settle()

            def norm(x_t, gain, dst):
                link(nc.vector.reciprocal(rstd[:, :], rms[:, :]))
                return nc.vector.scalar_tensor_tensor(dst, x_t, rstd[:, 0:1], gain[:, :], ALU.mult, ALU.mult)

            def top16(values, place_v, place_i, scratch):
                link(nc.vector.max(place_v[:, 0:8], values))
                tick(nc.vector.max_index(place_i[:, 0:8], place_v[:, 0:8], values))
                link(nc.vector.match_replace(scratch, place_v[:, 0:8], values, -BIG))
                link(nc.vector.max(place_v[:, 8:16], scratch))
                return nc.vector.max_index(place_i[:, 8:16], place_v[:, 8:16], scratch)

            def front(s, piece):
                l, t = STAGES[s]
                nkeys = (t + 1) * P
                if piece == 0:
                    dve.wait_ge(rms1_ready, s + 1)
                    dve.wait_ge(norms_in, 32 * (l + 1))
                    norm(x[:, t, :], gain_attn, h_attn).then_inc(h1_ready, 1)
                    if l == 0:
                        use = ("proj", s, 7)
                        mm.wait_full(dve, use)
                        ins = nc.vector.tensor_tensor(fz[:, 0, :], mm.bank(use)[:, 0:8], f_bias[:, :], ALU.add)
                        ins.then_inc(mm.freed(use), 1)
                        mm.wait_evacuated(dve, use)
                        link(nc.vector.tensor_scalar(fz[:, 1, :], fz[:, 0, :], -1.0, None, ALU.mult))
                        nc.vector.tensor_tensor(fz[:, 1, :], fz[:, 0, :], fz[:, 1, :], ALU.min).then_inc(fz_ready, 1)
                        link(nc.vector.tensor_scalar(fz[:, 0, :], fz[:, 0, :], 0.0, None, ALU.min))
                    nh = 32 if l == 0 else 18
                    dve.wait_ge(squares_ready, s + 1)
                    nc.vector.tensor_reduce(head_ss[:, 0:nh], aug[:, 0:nh, 0:HD], AX_X, ALU.add).then_inc(head_ss_ready, 1)
                    dve.wait_ge(head_rms_ready, s + 1)
                    link(nc.vector.reciprocal(head_ss[:, 0:nh], head_ss[:, 0:nh]))
                    link(nc.vector.tensor_tensor(
                        aug[:, 0:nh, 0:HD], raw[:, 0:nh * HD].rearrange("p (h d) -> p h d", d=HD),
                        head_ss[:, 0:nh].unsqueeze(2).to_broadcast([P, nh, HD]), ALU.mult))
                    spans = [(8 * i, 8) for i in range(4)] if l == 0 else [(0, 16), (16, 2)]
                    for i, (a, n) in enumerate(spans):
                        tick(nc.vector.tensor_tensor(aug[:, a:a + n, 0:HD], aug[:, a:a + n, 0:HD],
                                                     g_heads[l][:, i:i + 1, :].to_broadcast([P, n, HD]), ALU.mult))
                    if l == 0:
                        tick(nc.vector.tensor_scalar(gate[:, :], gate[:, :], 1.0, None, ALU.add))
                    settle()
                    if l == 0:
                        tick(nc.vector.reciprocal(gate[:, :], gate[:, :]))
                    n = 16 if l == 0 else 18
                    cos = cst[:, C_COS + ROT * t:C_COS + ROT * (t + 1)].unsqueeze(1).to_broadcast([P, n, ROT])
                    sin = cst[:, C_SIN + ROT * t:C_SIN + ROT * (t + 1)].unsqueeze(1).to_broadcast([P, n, ROT])
                    x1, x2 = aug[:, 0:n, 0:ROT], aug[:, 0:n, ROT:2 * ROT]
                    for i, (a, b) in enumerate(((x1, cos), (x2, sin), (x2, cos), (x1, sin))):
                        tick(nc.vector.tensor_tensor(rope_tmp[:, i, 0:n, :], a, b, ALU.mult))
                    settle()
                    last = nc.vector.tensor_tensor(x1, rope_tmp[:, 0, 0:n, :], rope_tmp[:, 1, 0:n, :], ALU.subtract)
                    last = nc.vector.tensor_tensor(x2, rope_tmp[:, 2, 0:n, :], rope_tmp[:, 3, 0:n, :], ALU.add)
                    if l == 0:
                        dve.wait_ge(fln_ready, s + 1)
                        nc.vector.tensor_tensor(log_f[:, t, :], fz[:, 0, :], fz[:, 3, :], ALU.subtract).then_inc(log_f_ready, 1)
                        use = ("F", s)
                        mm.wait_full(dve, use)
                        f = mm.bank(use)[:, 0:8].unsqueeze(2)
                        nc.vector.tensor_copy(aug[:, 16:24, HD:HD + 1], f)
                        last = nc.vector.tensor_scalar(aug[:, 24:32, HD + 1:HD + 2], f, -1.0, None, ALU.mult)
                        last.then_inc(mm.freed(use), 1)
                        nc.vector.memset(aug[:, 16:24, HD + 1:HD + 2], 1.0)
                        last = nc.vector.memset(aug[:, 24:32, HD:HD + 1], 1.0)
                    last.then_inc(aug_ready, 1)
                elif piece == 1:
                    mask = masks[l][:, 2 * P - nkeys:2 * P]
                    for j in range(HEADS):
                        use = ("S", s, j)
                        mm.wait_full(dve, use)
                        if j >= 2:
                            tp.wait_full(dve, ("PT", s, j - 2))
                        nc.vector.tensor_tensor_reduce(
                            out=probs[:, j % 2, 0:nkeys], in0=mm.bank(use)[:, 0:nkeys], in1=mask, scale=-1.0,
                            scalar=neg_sink[:, j:j + 1] if l == 1 else BIG, op0=ALU.add, op1=ALU.min,
                            accum_out=neg_max[:, j:j + 1]).then_inc(mm.freed(use), 1)
                        if j % 8 == 7:
                            i = j // 8
                            heads = slice(8 * i, 8 * i + 8)
                            if l == 1:
                                for i2 in (j - 1, j):
                                    mm.wait_evacuated(dve, ("S", s, i2))
                                nc.vector.tensor_tensor(sink_e[:, heads], sink[:, heads], neg_max[:, heads],
                                                        ALU.add).then_inc(sink_in_ready, 1)
                                dve.wait_ge(sink_e_ready, 2 * t + i + 1)
                                dve.wait_ge(probs_ready, HEADS * s + j + 1)
                                link(nc.vector.tensor_tensor(row_sum[:, heads], row_sum[:, heads], sink_e[:, heads], ALU.add))
                            dve.wait_ge(probs_ready, HEADS * s + j + 1)
                            link(nc.vector.reciprocal(row_sum[:, heads], row_sum[:, heads]))
                    for i in range(2):
                        dve.wait_ge(pv_done, HEADS * s + 8 * (i + 1))
                        heads = slice(8 * i, 8 * i + 8)
                        o = attended[:, CW * i:CW * i + CW].rearrange("p (h d) -> p h d", d=HD)
                        ins = nc.vector.tensor_tensor(
                            o, o_banks[i][:, :].rearrange("p (h d) -> p h d", d=HD),
                            row_sum[:, heads].unsqueeze(2).to_broadcast([P, 8, HD]), ALU.mult)
                        ins.then_inc(o_free, 1)
                    if l == 0:
                        dve.wait_ge(o_free, 2 * s + 2)
                        nc.vector.tensor_tensor(attended[:, CW:2 * CW], attended[:, CW:2 * CW], gate[:, :],
                                                ALU.mult).then_inc(gated, 1)
                    for c in range(2):
                        use = ("out", s, c)
                        mm.wait_full(dve, use)
                        xc = x[:, t, CW * c:CW * c + CW]
                        nc.vector.tensor_tensor(xc, xc, mm.bank(use)[:, :], ALU.add).then_inc(mm.freed(use), 1)
                else:
                    dve.wait_ge(rms2_ready, s + 1)
                    norm(x[:, t, :], gain_ffn, h_ffn[:, s % 2, :]).then_inc(h2_ready, 1)
                    for g in range(4):
                        use = ("sc", s, g)
                        mm.wait_full(dve, use)
                        for i in range(4):
                            n = 4 * g + i
                            last = top16(mm.bank(use)[:, i * NK:(i + 1) * NK], top_v[:, n, :], top_i[:, n, :], rest[:, 0:NK])
                            last.then_inc(*((mm.freed(use), 1) if i == 3 else (dve_step, 1)))
                            if i < 3:
                                steps[0] += 1
                        mm.wait_evacuated(dve, use)
                    for h in range(PH):
                        link(nc.vector.tensor_tensor(
                            cand[:, :].rearrange("p (a b) -> p a b", a=TK),
                            top_v[:, 2 * h, :].unsqueeze(2).to_broadcast([P, TK, TK]),
                            top_v[:, 2 * h + 1, :].unsqueeze(1).to_broadcast([P, TK, TK]), ALU.add))
                        tick(top16(cand[:, :], best_v[:, h, :], best_i[:, h, :], rest[:, :]))
                    settle()
                    flat_i = best_i[:, :, :].rearrange("p a b -> p (a b)")
                    link(nc.vector.tensor_copy(top_if, top_i[:, :, :]))
                    for half, (dst, op, by) in enumerate(((id_1, ALU.logical_shift_right, 4), (id_2, ALU.bitwise_and, 15))):
                        link(nc.vector.tensor_single_scalar(half_i, flat_i, by, op))
                        link(nc.vector.tensor_copy(half_f, half_i))
                        oh3 = onehot.rearrange("p (a b) -> p a b", b=TK)
                        oh4 = onehot.rearrange("p (h a b) -> p h a b", h=PH, b=TK)
                        link(nc.vector.tensor_tensor(oh3, half_f.unsqueeze(2).to_broadcast([P, PH * TK, TK]),
                                                     iota.unsqueeze(1).to_broadcast([P, PH * TK, TK]), ALU.is_equal))
                        names = top_if.rearrange("p (h two) b -> p h two b", two=2)[:, :, half, :]
                        link(nc.vector.tensor_tensor(oh4, oh4, names.unsqueeze(2).to_broadcast([P, PH, TK, TK]), ALU.mult))
                        link(nc.vector.tensor_reduce(dst, oh3, AX_X, ALU.add))
                    link(nc.vector.tensor_scalar(id_1, id_1, float(NK), float(l * EXPERTS), ALU.mult, ALU.add))
                    link(nc.vector.tensor_tensor(id_1, id_1, id_2, ALU.add))
                    link(nc.vector.tensor_copy(ids[:, PH * TK * s:PH * TK * (s + 1)], id_1))
                    link(nc.vector.tensor_copy(g_sum[:, :].unsqueeze(2), best_v[:, :, 0:1]))
                    nc.vector.tensor_tensor(best_v[:, :, :], best_v[:, :, :], g_sum[:, :].unsqueeze(2).to_broadcast([P, PH, TK]),
                                            ALU.subtract).then_inc(best_ready, 1)
                    dve.wait_ge(gexp_ready, s + 1)
                    link(nc.vector.tensor_reduce(g_sum[:, :], best_v[:, :, :], AX_X, ALU.add))
                    link(nc.vector.reciprocal(g_sum[:, :], g_sum[:, :]))
                    nc.vector.tensor_tensor(
                        gates[:, PH * TK * s:PH * TK * (s + 1)].rearrange("p (a b) -> p a b", a=PH),
                        best_v[:, :, :], g_sum[:, :].unsqueeze(2).to_broadcast([P, PH, TK]), ALU.mult).then_inc(ids_ready, 1)
                    dve.wait_ge(ids_ready, s + 1)

            def group(g, s):
                for k in range(TK):
                    dve.wait_ge(down_in[k % RING], 16 * (TK // RING * g + k // RING + 1))
                    nc.vector.scalar_tensor_tensor(
                        down_rows[:, k % RING, :], down_rows[:, k % RING, :], 1.0, h_ffn[:, s % 2, :], ALU.mult, ALU.mult,
                        accum_out=dots[:, k:k + 1]).then_inc(dots_done, 1)
                dve.wait_ge(gelu_done, g + 1)
                if not (isinstance(g, int) and g == 0):
                    dve.wait_ge(w_taken, g)
                nc.vector.tensor_tensor(w_next[:, :], gelus[:, :], gates[:, bass.ds(TK * g, TK)], ALU.mult).then_inc(w_ready, 1)

            dve.wait_ge(consts_in, 5 * 16)
            for g in (g_heads[0][:, 0, :], g_heads[0][:, 2, :], g_heads[1][:, 0, :]):
                link(nc.vector.tensor_scalar(g, g, SCALE, None, ALU.mult))
            link(nc.vector.tensor_scalar(neg_sink[:, :], sink[:, :], -1.0, None, ALU.mult))
            for piece in range(3):
                front(0, piece)
            group(0, 0)
            for s in range(4):
                for i, (a, b) in enumerate(SPLITS):
                    if b - a > 1:
                        with dve.Fori(PH * s + a + 1, PH * s + b + 1) as g:
                            group(g, s)
                    else:
                        group(PH * s + a + 1, s)
                    if s < 3 and i < 3:
                        front(s + 1, i)
                if s < 3:
                    group(PH * (s + 1), s + 1)


def kernel(x, attn_norm, ffn_norm, ev_w_in, ev_forget_bias, ev_q_norm_a, ev_k_norm_a,
           ev_q_norm_b, ev_k_norm_b, ev_w_out, od_w_in, od_q_norm, od_k_norm, od_sinks,
           od_w_out, peer_w_query, peer_sub_keys, peer_down, peer_up):
    import numpy as np
    import concourse.bacc as bacc
    from concourse.bass_utils import run_bass_kernel_spmd

    seq = np.arange(2 * P, dtype=np.float32)
    inv_freq = np.power(np.float32(500000.0), -np.arange(0, 2 * ROT, 2, dtype=np.float32) / np.float32(2 * ROT))
    ang = (seq[:, None] * inv_freq[None, :]).astype(np.float32)
    c = np.zeros((P, C_END), np.float32)
    i, j = np.arange(P)[:, None], np.arange(P)[None, :]
    c[:, C_ID:C_ID + P] = i == j
    c[:, C_M0 + P:C_M0 + 2 * P] = np.where(j <= i, 0.0, NEG_INF)
    c[:, C_M1 + P:C_M1 + 2 * P] = np.where(j <= i, 0.0, NEG_INF)
    c[:, C_M1:C_M1 + P] = np.where(j > i, 0.0, NEG_INF)
    c[:, C_TRI:C_TRI + P] = i <= j
    c[:, C_ONES:C_ONES + P] = 1.0
    for t in range(2):
        c[:, C_COS + ROT * t:C_COS + ROT * (t + 1)] = np.cos(ang[P * t:P * (t + 1)])
        c[:, C_SIN + ROT * t:C_SIN + ROT * (t + 1)] = np.sin(ang[P * t:P * (t + 1)])
    c[:, C_IOTA:C_IOTA + TK] = np.arange(TK)
    c[:, C_EPS] = EPS
    con = np.ascontiguousarray
    a = np.asarray
    arrays = {
        "x_in": con(a(x)[0]), "consts": c, "attn_norm": con(a(attn_norm)), "ffn_norm": con(a(ffn_norm)),
        "w_in0": con(a(ev_w_in)[0]), "fbias": con(a(ev_forget_bias)[0]),
        "head_gains0": np.stack([a(ev_q_norm_a)[0], a(ev_k_norm_a)[0], a(ev_q_norm_b)[0], a(ev_k_norm_b)[0]]),
        "w_out0": con(a(ev_w_out)[0]), "w_in1": con(a(od_w_in)[0]),
        "head_gains1": np.stack([a(od_q_norm)[0], a(od_k_norm)[0]]), "sinks": con(a(od_sinks)[0]),
        "w_out1": con(a(od_w_out)[0]), "w_query": con(a(peer_w_query)),
        "keys_t": con(a(peer_sub_keys).transpose(4, 0, 1, 2, 3).reshape(HD, 2, 2 * PH, NK)),
        "down": con(a(peer_down).reshape(2 * EXPERTS, D)), "up": con(a(peer_up).reshape(2 * EXPERTS, D)),
    }
    nc = bacc.Bacc("TRN2", target_bir_lowering=False, num_devices=1)
    args = [nc.dram_tensor(k, v.shape, mybir.dt.from_np(v.dtype), kind="ExternalInput").ap() for k, v in arrays.items()]
    args.append(nc.dram_tensor("out", (2 * P, D), F32, kind="ExternalOutput").ap())
    build(nc, *args)
    r = run_bass_kernel_spmd(nc, [arrays], core_ids=[0])
    return r.results[0]["out"].reshape(1, 2 * P, D)
```

```python
from contextlib import ExitStack

import concourse.bass as bass
from concourse import mybir

ALU = mybir.AluOpType
ACT = mybir.ActivationFunctionType
F32 = mybir.dt.float32
BF16 = mybir.dt.bfloat16
U32 = mybir.dt.uint32
AX_X = mybir.AxisListType.X

P = 128
D = 1024
KT = D // P
HD = 64
HEADS = 16
EPS = 1e-6
NEG_INF = -1e30
BIG = 3.0e38
SCALE = HD ** -0.5
ROT = 8
CW = 512
PH = 8
TK = 16
NK = 128
EXPERTS = NK * NK
STAGES = [(0, 0), (0, 1), (1, 0), (1, 1)]
RING = 8
DIAGS = RING
WSLOTS = 2
AUGW = HD + 2

C_ID, C_M0, C_TRI, C_ONES, C_M1, C_COS, C_SIN, C_IOTA, C_EPS, C_END = 0, 128, 384, 512, 640, 896, 912, 928, 944, 945

CHUNKS = [[(CW * c, CW) for c in range(7)] + [(7 * CW, 8)], [(0, CW), (CW, CW), (2 * CW, 256)]]
UNITS = PH * TK // RING
AHEAD = 2
PIECE_CHUNKS = [{"proj0": (0, 1), "proj1": (2, 3, 4), "proj2": (5, 6, 7)},
                {"proj0": (0,), "proj1": (1,), "proj2": (2,)}]

FRONT = ["norm", "proj0", "proj1", "proj2", "heads", "attn0", "attn1", "attn2", "attn3", "out", "ffn",
         "topk0", "topk1", "topk2", "topk3"]


def schedule():
    steps = [("front", 0, "norm"), ("front", 1, "norm")] + [("front", 0, p) for p in FRONT[1:12]]
    steps += [("chunks", 1, (5, 0, 1)), ("first dots",), ("chunks", 1, (3, 4, 7))]
    for s in range(4):
        steps.append(("open", s))
        if s == 0:
            pieces = [[(0, "topk1")], [(0, "topk2")], [(0, "topk3")]] + [[(1, p)] for p in FRONT[4:]]
            ends = [0, 1, 2] + list(range(3, 14))
        elif s < 3:
            pieces = [[(s + 1, "norm"), (s + 1, "proj0")]] + [[(s + 1, p)] for p in FRONT[2:]]
            ends = list(range(1, 15))
        else:
            pieces, ends = [], []
        at = 0
        for end, ps in zip(ends, pieces):
            if end > at:
                steps.append(("units", s, at, end))
            steps += [("front", f, p) for f, p in ps]
            at = end
        steps += [("units", s, at, UNITS - AHEAD)] * (at < UNITS - AHEAD) + [("close", s)]
    return steps


def companion(s, j):
    return ("proj", 1, {5: 6, 11: 2}[j]) if s == 0 and j in (5, 11) else None


def head_span(l, c):
    if l == 0:
        return {0: (0, 8, 0), 1: (8, 8, 1), 3: (16, 8, 2), 4: (24, 8, 3)}.get(c)
    return ((0, 8, 0), (8, 8, 0), (16, 2, 1))[c]


def bank_uses():
    mm, tp, chunks = [], [], []
    for step in SCHEDULE:
        if step[0] == "chunks":
            mm += [("proj", step[1], c) for c in step[2]]
        if step[0] == "open" and step[1] == 0:
            mm.append(("sc", 0, 1))
        if step[0] != "front":
            continue
        _, s, piece = step
        l = STAGES[s][0]
        if piece == "norm":
            tp += [("h1", s, i) for i in range(2)]
        elif piece in PIECE_CHUNKS[l]:
            mm += [("proj", s, c) for c in PIECE_CHUNKS[l][piece]]
        elif piece == "heads":
            mm += [("F", s)] * (l == 0)
            tp += [("qk", s, g) for g in range(8 if l == 0 else 5)]
        elif piece.startswith("attn"):
            first = 4 * int(piece[4])
            mm += [("S", s, first), ("S", s, first + 1)]
            for j in range(first, first + 4):
                tp.append(("PT", s, j))
                mm += [("S", s, j + 2)] * (j + 2 < first + 4) + [companion(s, j)] * bool(companion(s, j))
        elif piece == "out":
            tp += [("att", s, i) for i in range(2)]
            mm += [("out", s, c) for c in range(2)]
        elif piece == "ffn":
            tp += [("h2", s, i) for i in range(2)] + [("pq", s, g) for g in range(4)]
            mm += [("wq", s, c) for c in range(2)] + [("sc", s, 0)]
        elif piece in ("topk0", "topk1", "topk2") and (s, piece) != (0, "topk0"):
            mm.append(("sc", s, int(piece[4]) + 1))
    return mm, tp, [u for u in mm if u[0] in ("proj", "out", "wq")]


SCHEDULE = schedule()


def q_head(layer, j):
    return j if layer == 1 or j < 8 else 16 + j - 8


def k_head(layer, j):
    return 16 + j // 8 if layer == 1 else 8 + j if j < 8 else 24 + j - 8


def k_rows(layer, j):
    return HD if layer == 1 or j < 8 else AUGW


class Banks:

    def __init__(self, full, free, tensors, uses):
        self.full, self.free, self.tensors = full, free, tensors
        self.number = {u: n for n, u in enumerate(uses)}

    def bank(self, use):
        return self.tensors[self.number[use] % 2]

    def freed(self, use):
        return self.free[self.number[use] % 2]

    def wait_room(self, eng, use):
        n = self.number[use]
        if n >= 2:
            eng.wait_ge(self.free[n % 2], n // 2)

    def wait_full(self, eng, use):
        eng.wait_ge(self.full, self.number[use] + 1)

    def wait_evacuated(self, eng, use):
        n = self.number[use]
        eng.wait_ge(self.free[n % 2], n // 2 + 1)


def build(nc, x_in, consts, attn_norm, ffn_norm, w_in0, fbias, head_gains0, w_out0, w_in1,
          head_gains1, sinks, w_out1, w_query, keys_t, down, up, out):
    ctx = ExitStack()
    with ctx:
        def sb(name, shape, dt=F32):
            return ctx.enter_context(nc.sbuf_tensor(name, shape, dt))

        def sem(name):
            return ctx.enter_context(nc.semaphore(name))

        cst = sb("cst", [P, C_END])
        ident = cst[:, C_ID:C_ID + P]
        masks = [cst[:, C_M0:C_M0 + 2 * P], cst[:, C_M1:C_M1 + 2 * P]]
        tri = cst[:, C_TRI:C_TRI + P]
        ones = cst[:, C_ONES:C_ONES + P]
        iota = cst[:, C_IOTA:C_IOTA + TK]
        eps = cst[:, C_EPS:C_EPS + 1]
        down_rows = sb("down_rows", [P, RING, D])
        up_rows = sb("up_rows", [P, RING, D])
        diags = sb("diags", [P, DIAGS, P])
        x = sb("x", [P, 2, D])
        h_ffn = sb("h_ffn", [P, 2, D])
        gain_attn = sb("gain_attn", [P, D])
        gain_ffn = sb("gain_ffn", [P, D])
        act_t = sb("act_t", [P, KT, P])
        weights = sb("weights", [P, WSLOTS, KT, CW])
        keys = sb("keys", [HD, 2 * PH, NK])
        raw = sb("raw", [P, 2 * D])
        squares = raw[:, 0:CW].rearrange("p (h d) -> p h d", d=HD)
        h_attn = raw[:, 0:D]
        h1_t = [h_ffn[:, 1, :].rearrange("p (a b) -> p a b", a=KT) if s == 1 else act_t for s in range(4)]
        attended = raw[:, 0:D]
        queries = raw[:, D:2 * D]
        aug = sb("aug", [P, 32, AUGW])
        q_t = sb("q_t", [AUGW, HEADS, P])
        k_t = sb("k_t", [AUGW, HEADS, 2 * P])
        v = sb("v", [P, 2, D])
        gate = sb("gate", [P, 2, CW])
        probs = sb("probs", [P, 2, 2 * P])
        onehot = probs[:, :, :].rearrange("p a b -> p (a b)")
        probs_t = sb("probs_t", [P, 2, 2 * P])
        ids = sb("ids", [P, 4 * PH * TK], U32)
        gates = sb("gates", [P, 4 * PH * TK])
        down_ids = sb("down_ids", [P, 2, RING], U32)
        up_ids = sb("up_ids", [P, 2, RING], U32)
        dots = sb("dots", [P, RING])
        gelus = sb("gelus", [P, RING])
        w_now = sb("w_now", [P, RING])
        g_heads = [sb("g_heads0", [P, 4, HD]), sb("g_heads1", [P, 2, HD])]
        sink = sb("sink", [P, HEADS])
        f_bias = sb("f_bias", [P, 8])
        sumsq = sb("sumsq", [P, 1])
        rms = sb("rms", [P, 1])
        rstd = sb("rstd", [P, 1])
        head_ss = sb("head_ss", [P, 8])
        rope_tmp = raw[:, 0:4 * 18 * ROT].rearrange("p (a h r) -> p a h r", a=4, h=18)
        fz = sb("fz", [P, 2, 4, 8])
        log_f = sb("log_f", [P, 2, 8])
        neg_max = sb("neg_max", [P, HEADS])
        row_sum = sb("row_sum", [P, HEADS])
        sink_e = sb("sink_e", [P, HEADS])
        neg_sink = sb("neg_sink", [P, HEADS])
        top_v = sb("top_v", [P, 4, TK])
        top_i = sb("top_i", [P, 4, TK], U32)
        rest = sb("rest", [P, TK * TK])
        cand = sb("cand", [P, TK * TK])
        best_v = sb("best_v", [P, PH, TK])
        best_i = sb("best_i", [P, 2, TK], U32)
        top_if = sb("top_if", [P, 4, TK])
        half_i = sb("half_i", [P, 2 * TK], U32)
        half_f = sb("half_f", [P, 2 * TK])
        id_1 = sb("id_1", [P, 2 * TK])
        id_2 = sb("id_2", [P, 2 * TK])
        g_sum = sb("g_sum", [P, 2])

        def bank(name):
            return ctx.enter_context(nc.psum_tensor(name, [P, CW], F32))

        acc = [bank("acc0"), bank("acc1")]
        mm_banks = [bank("mm0"), bank("mm1")]
        tp_banks = [bank("tp0"), bank("tp1")]
        o_banks = [bank("o0"), bank("o1")]

        consts_in = sem("consts_in")
        x_in_sem = [sem("x_in0"), sem("x_in1")]
        attn_gain_in = sem("attn_gain_in")
        norms_in = sem("norms_in")
        small_in = sem("small_in")
        keys_in = sem("keys_in")
        weights_in = [sem(f"weights_in{i}") for i in range(WSLOTS)]
        mm_full, mm_free = sem("mm_full"), [sem("mm_free0"), sem("mm_free1")]
        tp_full, tp_free = sem("tp_full"), [sem("tp_free0"), sem("tp_free1")]
        dve_step = sem("dve_step")
        ss1_ready, rms1_ready, h1_ready = sem("ss1_ready"), sem("rms1_ready"), sem("h1_ready")
        rms2_ready, head_ss_ready, head_rms_ready = sem("rms2_ready"), sem("head_ss_ready"), sem("head_rms_ready")
        squares_ready, aug_ready = sem("squares_ready"), sem("aug_ready")
        fz_ready, fe_ready, fln_ready = sem("fz_ready"), sem("fe_ready"), sem("fln_ready")
        log_f_ready, f_ready = sem("log_f_ready"), sem("f_ready")
        probs_ready = sem("probs_ready")
        pv_done, o_free = sem("pv_done"), sem("o_free")
        sink_in_ready, sink_e_ready = sem("sink_in_ready"), sem("sink_e_ready")
        gated = sem("gated")
        ss2_ready, h2_ready = sem("ss2_ready"), sem("h2_ready")
        best_ready, gexp_ready, ids_ready = sem("best_ready"), sem("gexp_ready"), sem("ids_ready")
        down_in = [sem(f"down_in{i}") for i in range(RING)]
        up_in = [sem(f"up_in{i}") for i in range(RING)]
        down_staged, up_staged = sem("down_staged"), sem("up_staged")
        slots_claimed = sem("slots_claimed")
        dots_done, gelu_done = sem("dots_done"), sem("gelu_done")
        w_ready, w_taken = sem("w_ready"), sem("w_taken")
        diag_ready, up_done = sem("diag_ready"), sem("up_done")
        x_out_ready, out_written = sem("x_out_ready"), sem("out_written")

        mm_uses, tp_uses, chunk_list = bank_uses()
        head_chunks = [u for u in chunk_list if u[0] == "proj" and head_span(STAGES[u[1]][0], u[2])]
        norm_no = {u: n for n, u in enumerate(head_chunks)}
        mm = Banks(mm_full, mm_free, mm_banks, mm_uses)
        tp = Banks(tp_full, tp_free, tp_banks, tp_uses)
        chunk_no = {c: n for n, c in enumerate(chunk_list)}

        def chunk_cols(use):
            kind, s, c = use
            return CHUNKS[STAGES[s][0]][c] if kind == "proj" else (CW * c, CW)

        def chunk_source(use):
            kind, s, c = use
            l = STAGES[s][0]
            a, w = chunk_cols(use)
            m = {"proj": (w_in0, w_in1), "out": (w_out0, w_out1), "wq": (w_query[0], w_query[1])}[kind][l]
            return m[:, a:a + w].rearrange("(kt p) n -> p kt n", p=P)

        def qk_group(s, g):
            l = STAGES[s][0]
            if g < 4:
                return [(q_head(l, j), j, k_rows(l, j)) for j in range(4 * g, 4 * g + 4)]
            if l == 0:
                return [(k_head(l, j), j, k_rows(l, j)) for j in range(4 * (g - 4), 4 * (g - 4) + 4)]
            return [(16 + i, i, HD) for i in range(2)]

        def v_cols(l, j):
            return slice(HD * j, HD * j + HD) if l == 0 else slice(HD * (j // 8), HD * (j // 8) + HD)

        def wait_residual(eng, s):
            for c in range(2):
                mm.wait_evacuated(eng, ("out", s, c))

        block = ctx.enter_context(nc.Block())

        @block.sync
        def _(sp):
            def layer_loads(l):
                sp.dma_start(gain_ffn[:, :], ffn_norm[l].partition_broadcast(P)).then_inc(norms_in, 16)
                sp.dma_start(keys[:, :, :], keys_t[:, l]).then_inc(keys_in, 16)

            def gain_load(l):
                sp.dma_start(gain_attn[:, :], attn_norm[l].partition_broadcast(P)).then_inc(attn_gain_in, 16)

            sp.dma_start(x[:, 0, :], x_in[0:P, :]).then_inc(x_in_sem[0], 16)
            gain_load(0)
            for n, use in enumerate(chunk_list):
                if use == ("proj", 2, 0):
                    sp.wait_ge(h2_ready, 2)
                    mm.wait_full(sp, ("sc", 1, 3))
                    gain_load(1)
                    layer_loads(1)
                if n >= WSLOTS:
                    mm.wait_full(sp, chunk_list[n - WSLOTS])
                w = chunk_cols(use)[1]
                sp.dma_start(weights[:, n % WSLOTS, :, 0:w], chunk_source(use)).then_inc(weights_in[n % WSLOTS], 16)
                if n == 0:
                    sp.dma_start(x[:, 1, :], x_in[P:2 * P, :]).then_inc(x_in_sem[1], 16)
                if use == ("out", 0, 0):
                    layer_loads(0)
            for t in range(2):
                sp.wait_ge(x_out_ready, 2 * (2 + t) + 2)
                sp.dma_start(out[t * P:(t + 1) * P, :], x[:, t, :]).then_inc(out_written, 16)
            sp.wait_ge(out_written, 32)

        @block.gpsimd
        def _(pool):
            def gather(table, rows, id_column, k, landed):
                pool.indirect_dma_start(
                    out=rows[:, k, :], out_offset=None, in_=table,
                    in_offset=bass.IndirectOffsetOnAxis(ap=id_column, axis=0)).then_inc(landed[k], 16)

            def slot(n, k, parity, table, rows, ids_now, staged, used, landed):
                if not (isinstance(n, int) and n <= 0):
                    pool.wait_ge(used, RING * n + k + 1 - RING)
                    pool.sem_inc(slots_claimed, 1)
                if k == 0:
                    nc.gpsimd.tensor_copy(ids_now[:, parity, :], ids[:, bass.ds(RING * n, RING)]).then_inc(staged, 1)
                    pool.wait_ge(staged, n + 1)
                    pool.sem_inc(slots_claimed, 1)
                gather(table, rows, ids_now[:, parity, k:k + 1], k, landed)

            def down_slot(n, k, parity):
                slot(n, k, parity, down, down_rows, down_ids, down_staged, dots_done, down_in)

            def up_slot(n, k, parity):
                slot(n, k, parity, up, up_rows, up_ids, up_staged, up_done, up_in)

            def head(g, last=False):
                if not last:
                    pool.wait_ge(ids_ready, g + 2)
                for half in range(2):
                    n = 2 * g + half
                    for k in range(RING):
                        if not last:
                            down_slot(n + AHEAD, k, half)
                        up_slot(n, k, half)

            pool.wait_ge(ids_ready, 1)
            for n in range(AHEAD):
                for k in range(RING):
                    down_slot(n, k, n)
            head(0)
            with pool.Fori(1, 4 * PH - 1) as g:
                head(g)
            head(4 * PH - 1, last=True)

        @block.scalar
        def _(act):
            def evacuate(banks, use, dst, src):
                banks.wait_full(act, use)
                nc.scalar.copy(dst, src).then_inc(banks.freed(use), 1)

            def transposed(kind, s, dst=act_t):
                for i in range(2):
                    evacuate(tp, (kind, s, i), dst[:, 4 * i:4 * i + 4, :],
                             tp.bank((kind, s, i))[:, :].rearrange("p (a b) -> p a b", a=4))

            def projection(use):
                _, s, c = use
                l, t = STAGES[s]
                b = mm.bank(use)
                heads_of = b[:, :].rearrange("p (h d) -> p h d", d=HD)
                if l == 1 and c == 2:
                    mm.wait_full(act, use)
                    nc.scalar.copy(v[:, t, 0:P], b[:, P:2 * P])
                    evacuate(mm, use, aug[:, 16:18, 0:HD], heads_of[:, 0:2, :])
                elif head_span(l, c):
                    a, n, _ = head_span(l, c)
                    evacuate(mm, use, aug[:, a:a + n, 0:HD], heads_of)
                elif c in (2, 5):
                    i = c // 5
                    evacuate(mm, use, v[:, t, CW * i:CW * i + CW], b[:, :])
                elif c == 6:
                    mm.wait_full(act, use)
                    nc.scalar.activation(gate[:, t, :], b[:, :], ACT.Exp, scale=-1.0).then_inc(mm.freed(use), 1)
                if head_span(l, c):
                    a, n, _ = head_span(l, c)
                    mm.wait_evacuated(act, use)
                    nc.scalar.activation(squares[:, 0:n, :], aug[:, a:a + n, 0:HD], ACT.Square).then_inc(squares_ready, 1)
                    act.wait_ge(head_ss_ready, norm_no[use] + 1)
                    nc.scalar.activation(head_ss[:, 0:n], head_ss[:, 0:n], ACT.Sqrt, scale=1.0 / HD,
                                         bias=eps).then_inc(head_rms_ready, 1)

            def front(s, piece):
                l, t = STAGES[s]
                nkeys = (t + 1) * P
                if piece == "norm":
                    if l == 0:
                        act.wait_ge(x_in_sem[t], 16)
                    else:
                        act.wait_ge(x_out_ready, 2 * (s - 2) + 2)
                    if s == 1:
                        tp.wait_full(act, ("h1", 0, 1))
                    elif s:
                        act.wait_ge(ids_ready, PH * s)
                    nc.scalar.activation(h_attn, x[:, t, :], ACT.Square, accum_out=sumsq[:, :]).then_inc(ss1_ready, 1)
                    act.wait_ge(ss1_ready, s + 1)
                    nc.scalar.activation(rms[:, :], sumsq[:, :], ACT.Sqrt, scale=1.0 / D, bias=eps).then_inc(rms1_ready, 1)
                    if s >= 2:
                        mm.wait_full(act, ("wq", s - 1, 1))
                    transposed("h1", s, h1_t[s])
                elif piece in PIECE_CHUNKS[l]:
                    for c in PIECE_CHUNKS[l][piece]:
                        projection(("proj", s, c))
                elif piece == "heads":
                    if s == 1:
                        act.wait_ge(ids_ready, PH)
                    if l == 0:
                        act.wait_ge(fz_ready, s + 1)
                        nc.scalar.activation(fz[:, t, 2, :], fz[:, t, 1, :], ACT.Exp).then_inc(fe_ready, 1)
                        act.wait_ge(fe_ready, s + 1)
                        nc.scalar.activation(fz[:, t, 3, :], fz[:, t, 2, :], ACT.Ln, bias=1.0).then_inc(fln_ready, 1)
                    for g in range(8 if l == 0 else 5):
                        heads = qk_group(s, g)
                        use = ("qk", s, g)
                        n, rows = len(heads), heads[0][2]
                        j = heads[0][1]
                        src = tp.bank(use)[0:rows, 0:n * P].rearrange("p (a b) -> p a b", a=n)
                        dst = q_t[0:rows, j:j + n, :] if g < 4 else k_t[0:rows, j:j + n, t * P:(t + 1) * P]
                        evacuate(tp, use, dst, src)
                elif piece.startswith("attn"):
                    first = 4 * int(piece[4])
                    def transposed_probs(j):
                        if j >= 2 or s:
                            act.wait_ge(pv_done, HEADS * s + j - 1)
                        evacuate(tp, ("PT", s, j), probs_t[:, j % 2, 0:nkeys], tp.bank(("PT", s, j))[:, 0:nkeys])

                    for j in range(first, first + 4):
                        mm.wait_evacuated(act, ("S", s, j))
                        nc.scalar.activation(probs[:, j % 2, 0:nkeys], probs[:, j % 2, 0:nkeys], ACT.Exp,
                                             scale=-1.0, bias=neg_max[:, j:j + 1],
                                             accum_out=row_sum[:, j:j + 1]).then_inc(probs_ready, 1)
                        if j > first:
                            transposed_probs(j - 1)
                            if companion(s, j - 1):
                                projection(companion(s, j - 1))
                        if l == 1 and j % 8 == 7:
                            i = j // 8
                            act.wait_ge(sink_in_ready, 2 * t + i + 1)
                            nc.scalar.activation(sink_e[:, 8 * i:8 * i + 8], sink_e[:, 8 * i:8 * i + 8],
                                                 ACT.Exp).then_inc(sink_e_ready, 1)
                    transposed_probs(first + 3)
                    if companion(s, first + 3):
                        projection(companion(s, first + 3))
                elif piece == "out":
                    mm.wait_full(act, ("proj", s, len(CHUNKS[l]) - 1))
                    transposed("att", s)
                elif piece == "ffn":
                    wait_residual(act, s)
                    nc.scalar.activation(queries, x[:, t, :], ACT.Square, accum_out=sumsq[:, :]).then_inc(ss2_ready, 1)
                    act.wait_ge(ss2_ready, s + 1)
                    nc.scalar.activation(rms[:, :], sumsq[:, :], ACT.Sqrt, scale=1.0 / D, bias=eps).then_inc(rms2_ready, 1)
                    mm.wait_full(act, ("out", s, 1))
                    transposed("h2", s)
                    for c in range(2):
                        evacuate(mm, ("wq", s, c), queries[:, CW * c:CW * c + CW], mm.bank(("wq", s, c))[:, :])
                    for g in range(4):
                        evacuate(tp, ("pq", s, g), q_t[0:HD, 4 * g:4 * g + 4, :],
                                 tp.bank(("pq", s, g))[0:HD, :].rearrange("p (a b) -> p a b", a=4))
                elif piece.startswith("topk"):
                    b = int(piece[4])
                    pair = best_v[:, 2 * b:2 * b + 2, :]
                    act.wait_ge(best_ready, 4 * s + b + 1)
                    nc.scalar.activation(pair, pair, ACT.Exp).then_inc(gexp_ready, 1)

            def gelu(u):
                act.wait_ge(dots_done, RING * (u + 1))
                nc.scalar.activation(gelus[:, :], dots[:, :], ACT.Gelu).then_inc(gelu_done, 1)

            def unit(u, with_down=True):
                act.wait_ge(w_ready, u + 1)
                if not (isinstance(u, int) and u == 0):
                    act.wait_ge(diag_ready, RING * u)
                nc.scalar.copy(w_now[:, :], gates[:, bass.ds(RING * u, RING)]).then_inc(w_taken, 1)
                act.wait_ge(w_taken, u + 1)
                for k in range(RING):
                    if not (isinstance(u, int) and RING * u + k + 1 - DIAGS <= 0):
                        act.wait_ge(up_done, RING * u + k + 1 - DIAGS)
                    nc.scalar.activation(diags[:, k, :], ident, ACT.Copy, scale=w_now[:, k:k + 1]).then_inc(diag_ready, 1)
                if with_down:
                    gelu(u + AHEAD)

            act.dma_start(cst[:, :], consts).then_inc(consts_in, 16)
            act.dma_start(g_heads[0][:, :, :], head_gains0.partition_broadcast(P)).then_inc(small_in, 16)
            act.dma_start(g_heads[1][:, :, :], head_gains1.partition_broadcast(P)).then_inc(small_in, 16)
            act.dma_start(sink[:, :], sinks.partition_broadcast(P)).then_inc(small_in, 16)
            act.dma_start(f_bias[:, :], fbias.partition_broadcast(P)).then_inc(small_in, 16)
            act.wait_ge(consts_in, 16)
            for step in SCHEDULE:
                if step[0] == "front":
                    front(*step[1:])
                elif step[0] == "chunks":
                    for c in step[2]:
                        projection(("proj", step[1], c))
                elif step[0] == "first dots":
                    for u in range(AHEAD):
                        gelu(u)
                elif step[0] == "units":
                    s, a, b = step[1:]
                    a, b = UNITS * s + a, UNITS * s + b
                    if a == 0:
                        unit(0)
                        a = 1
                    if b - a > 1:
                        with act.Fori(a, b) as u:
                            unit(u)
                    elif b > a:
                        unit(a)
                elif step[0] == "close":
                    s = step[1]
                    for u in range(UNITS * (s + 1) - AHEAD, UNITS * (s + 1)):
                        unit(u, with_down=s < 3)
                    act.wait_ge(up_done, PH * TK * (s + 1))
                    for c in range(2):
                        nc.scalar.copy(x[:, STAGES[s][1], CW * c:CW * c + CW], acc[c][:, :]).then_inc(x_out_ready, 1)

        @block.tensor
        def _(pe):
            def transposes(kind, s, src):
                for i in range(2):
                    use = (kind, s, i)
                    tp.wait_room(pe, use)
                    for k in range(4):
                        last = nc.tensor.transpose(tp.bank(use)[:, k * P:(k + 1) * P],
                                                   src[:, (4 * i + k) * P:(4 * i + k + 1) * P], ident)
                    last.then_inc(tp_full, 1)

            def project(use):
                n = chunk_no[use]
                w = chunk_cols(use)[1]
                pe.wait_ge(weights_in[n % WSLOTS], 16 * (n // WSLOTS + 1))
                mm.wait_room(pe, use)
                tokens = h1_t[use[1]] if use[0] == "proj" else act_t
                for k in range(KT):
                    last = nc.tensor.matmul(mm.bank(use)[:, 0:w], tokens[:, k, :], weights[:, n % WSLOTS, k, 0:w],
                                            start=(k == 0), stop=(k == KT - 1))
                last.then_inc(mm_full, 1)

            def key_scores(s, g):
                use = ("sc", s, g)
                tp.wait_evacuated(pe, ("pq", s, g))
                mm.wait_room(pe, use)
                for i in range(4):
                    last = nc.tensor.matmul(mm.bank(use)[:, i * NK:(i + 1) * NK], q_t[0:HD, 4 * g + i, :],
                                            keys[:, 4 * g + i, :], start=True, stop=True)
                last.then_inc(mm_full, 1)

            def front(s, piece):
                l, t = STAGES[s]
                nkeys = (t + 1) * P
                if piece == "norm":
                    pe.wait_ge(h1_ready, s + 1)
                    transposes("h1", s, h_attn)
                    for i in range(2):
                        tp.wait_evacuated(pe, ("h1", s, i))
                elif piece in PIECE_CHUNKS[l]:
                    for c in PIECE_CHUNKS[l][piece]:
                        project(("proj", s, c))
                elif piece == "heads":
                    if l == 0:
                        use = ("F", s)
                        pe.wait_ge(log_f_ready, s + 1)
                        mm.wait_room(pe, use)
                        if t:
                            nc.tensor.matmul(mm.bank(use)[:, 0:8], ones, log_f[:, 0, :], start=True, stop=False)
                        nc.tensor.matmul(mm.bank(use)[:, 0:8], tri, log_f[:, t, :], start=(t == 0),
                                         stop=True).then_inc(mm_full, 1)
                    pe.wait_ge(aug_ready, s + 1)
                    for g in range(8 if l == 0 else 5):
                        use = ("qk", s, g)
                        tp.wait_room(pe, use)
                        for i, (place, _, rows) in enumerate(qk_group(s, g)):
                            last = nc.tensor.transpose(tp.bank(use)[0:rows, i * P:(i + 1) * P], aug[:, place, 0:rows], ident)
                        last.then_inc(tp_full, 1)
                elif piece.startswith("attn"):
                    first = 4 * int(piece[4])
                    for g in range(8 if l == 0 else 5):
                        tp.wait_evacuated(pe, ("qk", s, g))

                    def scores(j):
                        use = ("S", s, j)
                        rows = k_rows(l, j)
                        mm.wait_room(pe, use)
                        kj = j if l == 0 else j // 8
                        nc.tensor.matmul(mm.bank(use)[:, 0:nkeys], q_t[0:rows, j, :], k_t[0:rows, kj, 0:nkeys],
                                         start=True, stop=True).then_inc(mm_full, 1)

                    def values(j):
                        use = ("PT", s, j)
                        tp.wait_evacuated(pe, use)
                        if j % 8 == 0 and s:
                            pe.wait_ge(o_free, 2 * (s - 1) + j // 8 + 1)
                        o = o_banks[j // 8][:, (j % 8) * HD:(j % 8 + 1) * HD]
                        for i in range(t + 1):
                            last = nc.tensor.matmul(o, probs_t[:, j % 2, i * P:(i + 1) * P], v[:, i, v_cols(l, j)],
                                                    start=(i == 0), stop=(i == t))
                        last.then_inc(pv_done, 1)

                    scores(first)
                    scores(first + 1)
                    for j in range(first, first + 4):
                        use = ("PT", s, j)
                        tp.wait_room(pe, use)
                        pe.wait_ge(probs_ready, HEADS * s + j + 1)
                        for i in range(t + 1):
                            last = nc.tensor.transpose(tp.bank(use)[:, i * P:(i + 1) * P],
                                                       probs[:, j % 2, i * P:(i + 1) * P], ident)
                        last.then_inc(tp_full, 1)
                        if j + 2 < first + 4:
                            scores(j + 2)
                        if j > first:
                            values(j - 1)
                        if companion(s, j):
                            project(companion(s, j))
                    values(first + 3)
                elif piece == "out":
                    pe.wait_ge(o_free, 2 * s + 2)
                    if l == 0:
                        pe.wait_ge(gated, s + 1)
                    transposes("att", s, attended)
                    for i in range(2):
                        tp.wait_evacuated(pe, ("att", s, i))
                    for c in range(2):
                        project(("out", s, c))
                elif piece == "ffn":
                    pe.wait_ge(h2_ready, s + 1)
                    transposes("h2", s, h_ffn[:, s % 2, :])
                    for i in range(2):
                        tp.wait_evacuated(pe, ("h2", s, i))
                    for c in range(2):
                        project(("wq", s, c))
                    for c in range(2):
                        mm.wait_evacuated(pe, ("wq", s, c))
                    for g in range(4):
                        use = ("pq", s, g)
                        tp.wait_room(pe, use)
                        for i in range(4):
                            last = nc.tensor.transpose(tp.bank(use)[0:HD, i * P:(i + 1) * P],
                                                       queries[:, (4 * g + i) * HD:(4 * g + i + 1) * HD], ident)
                        last.then_inc(tp_full, 1)
                    pe.wait_ge(keys_in, 16 * (l + 1))
                    key_scores(s, 0)
                elif piece in ("topk0", "topk1", "topk2") and (s, piece) != (0, "topk0"):
                    key_scores(s, int(piece[4]) + 1)

            def residual(s):
                wait_residual(pe, s)
                if s:
                    pe.wait_ge(x_out_ready, 2 * s)
                for c in range(2):
                    nc.tensor.matmul(acc[c][:, :], ident, x[:, STAGES[s][1], CW * c:CW * c + CW], start=True, stop=False,
                                     skip_group_check=True)

            def unit(u, last=False):
                for k in range(RING):
                    pe.wait_ge(diag_ready, RING * u + k + 1)
                    pe.wait_ge(up_in[k], 16 * (u + 1))
                    for c in range(2):
                        ins = nc.tensor.matmul(acc[c][:, :], diags[:, k, :], up_rows[:, k, CW * c:CW * c + CW],
                                               start=False, stop=(last and k == RING - 1), skip_group_check=True)
                    ins.then_inc(up_done, 1)

            pe.wait_ge(consts_in, 16)
            for step in SCHEDULE:
                if step[0] == "front":
                    front(*step[1:])
                elif step[0] == "chunks":
                    for c in step[2]:
                        project(("proj", step[1], c))
                elif step[0] == "open":
                    if step[1] == 0:
                        key_scores(0, 1)
                    residual(step[1])
                elif step[0] == "units":
                    s, a, b = step[1:]
                    a, b = UNITS * s + a, UNITS * s + b
                    if b > a + 1:
                        with pe.Fori(a, b) as u:
                            unit(u)
                    else:
                        unit(a)
                elif step[0] == "close":
                    s = step[1]
                    for u in range(UNITS * (s + 1) - AHEAD, UNITS * (s + 1)):
                        unit(u, last=u == UNITS * (s + 1) - 1)

        @block.vector
        def _(dve):
            steps = [0]

            def tick(ins):
                steps[0] += 1
                return ins.then_inc(dve_step, 1)

            def settle():
                dve.wait_ge(dve_step, steps[0])

            def link(ins):
                tick(ins)
                settle()

            def norm(x_t, gain, dst):
                link(nc.vector.reciprocal(rstd[:, :], rms[:, :]))
                return nc.vector.scalar_tensor_tensor(dst, x_t, rstd[:, 0:1], gain[:, :], ALU.mult, ALU.mult)

            def top16(values, place_v, place_i, scratch):
                link(nc.vector.max(place_v[:, 0:8], values))
                tick(nc.vector.max_index(place_i[:, 0:8], place_v[:, 0:8], values))
                link(nc.vector.match_replace(scratch, place_v[:, 0:8], values, -BIG))
                link(nc.vector.max(place_v[:, 8:16], scratch))
                return nc.vector.max_index(place_i[:, 8:16], place_v[:, 8:16], scratch)

            def projection(use):
                _, s, c = use
                l = STAGES[s][0]
                if head_span(l, c):
                    a, n, gain = head_span(l, c)
                    dve.wait_ge(squares_ready, norm_no[use] + 1)
                    nc.vector.tensor_reduce(head_ss[:, 0:n], squares[:, 0:n, :], AX_X, ALU.add).then_inc(head_ss_ready, 1)
                    dve.wait_ge(head_rms_ready, norm_no[use] + 1)
                    link(nc.vector.reciprocal(head_ss[:, 0:n], head_ss[:, 0:n]))
                    heads = aug[:, a:a + n, 0:HD]
                    link(nc.vector.tensor_tensor(heads, heads, head_ss[:, 0:n].unsqueeze(2).to_broadcast([P, n, HD]), ALU.mult))
                    link(nc.vector.tensor_tensor(heads, heads, g_heads[l][:, gain:gain + 1, :].to_broadcast([P, n, HD]), ALU.mult))
                if (l, c) != (0, 7):
                    return
                mm.wait_full(dve, use)
                nc.vector.tensor_tensor(fz[:, STAGES[s][1], 0, :], mm.bank(use)[:, 0:8], f_bias[:, :],
                                        ALU.add).then_inc(mm.freed(use), 1)
                mm.wait_evacuated(dve, use)

            def front(s, piece):
                l, t = STAGES[s]
                nkeys = (t + 1) * P
                if piece == "norm":
                    dve.wait_ge(rms1_ready, s + 1)
                    dve.wait_ge(attn_gain_in, 16 * (l + 1))
                    norm(x[:, t, :], gain_attn, h_attn).then_inc(h1_ready, 1)
                    if s == 1:
                        dve.wait_ge(small_in, 4 * 16)
                        for g in (g_heads[0][:, 0, :], g_heads[0][:, 2, :], g_heads[1][:, 0, :]):
                            link(nc.vector.tensor_scalar(g, g, SCALE, None, ALU.mult))
                        link(nc.vector.tensor_scalar(neg_sink[:, :], sink[:, :], -1.0, None, ALU.mult))
                elif piece in PIECE_CHUNKS[l]:
                    for c in PIECE_CHUNKS[l][piece]:
                        projection(("proj", s, c))
                elif piece == "heads":
                    if l == 0:
                        z, neg, low = fz[:, t, 0, :], fz[:, t, 1, :], fz[:, t, 0, :]
                        link(nc.vector.tensor_scalar(neg, z, -1.0, None, ALU.mult))
                        nc.vector.tensor_tensor(neg, z, neg, ALU.min).then_inc(fz_ready, 1)
                        link(nc.vector.tensor_scalar(low, z, 0.0, None, ALU.min))
                    n = 16 if l == 0 else 18
                    cos = cst[:, C_COS + ROT * t:C_COS + ROT * (t + 1)].unsqueeze(1).to_broadcast([P, n, ROT])
                    sin = cst[:, C_SIN + ROT * t:C_SIN + ROT * (t + 1)].unsqueeze(1).to_broadcast([P, n, ROT])
                    x1, x2 = aug[:, 0:n, 0:ROT], aug[:, 0:n, ROT:2 * ROT]
                    for i, (a, b) in enumerate(((x1, cos), (x2, sin), (x2, cos), (x1, sin))):
                        tick(nc.vector.tensor_tensor(rope_tmp[:, i, 0:n, :], a, b, ALU.mult))
                    settle()
                    last = nc.vector.tensor_tensor(x1, rope_tmp[:, 0, 0:n, :], rope_tmp[:, 1, 0:n, :], ALU.subtract)
                    last = nc.vector.tensor_tensor(x2, rope_tmp[:, 2, 0:n, :], rope_tmp[:, 3, 0:n, :], ALU.add)
                    if l == 0:
                        dve.wait_ge(fln_ready, s + 1)
                        nc.vector.tensor_tensor(log_f[:, t, :], fz[:, t, 0, :], fz[:, t, 3, :], ALU.subtract).then_inc(log_f_ready, 1)
                        use = ("F", s)
                        mm.wait_full(dve, use)
                        f = mm.bank(use)[:, 0:8].unsqueeze(2)
                        nc.vector.tensor_copy(aug[:, 16:24, HD:HD + 1], f)
                        last = nc.vector.tensor_scalar(aug[:, 24:32, HD + 1:HD + 2], f, -1.0, None, ALU.mult)
                        last.then_inc(mm.freed(use), 1)
                        nc.vector.memset(aug[:, 16:24, HD + 1:HD + 2], 1.0)
                        last = nc.vector.memset(aug[:, 24:32, HD:HD + 1], 1.0)
                    last.then_inc(aug_ready, 1)
                    if l == 0:
                        mm.wait_evacuated(dve, ("proj", s, 6))
                        link(nc.vector.tensor_scalar(gate[:, t, :], gate[:, t, :], 1.0, None, ALU.add))
                        link(nc.vector.reciprocal(gate[:, t, :], gate[:, t, :]))
                elif piece.startswith("attn"):
                    first = 4 * int(piece[4])
                    mask = masks[l][:, 2 * P - nkeys:2 * P]
                    for j in range(first, first + 4):
                        use = ("S", s, j)
                        mm.wait_full(dve, use)
                        if j >= 2:
                            tp.wait_full(dve, ("PT", s, j - 2))
                        nc.vector.tensor_tensor_reduce(
                            out=probs[:, j % 2, 0:nkeys], in0=mm.bank(use)[:, 0:nkeys], in1=mask, scale=-1.0,
                            scalar=neg_sink[:, j:j + 1] if l == 1 else BIG, op0=ALU.add, op1=ALU.min,
                            accum_out=neg_max[:, j:j + 1]).then_inc(mm.freed(use), 1)
                        if j % 8 == 7:
                            i = j // 8
                            heads = slice(8 * i, 8 * i + 8)
                            if l == 1:
                                for i2 in (j - 1, j):
                                    mm.wait_evacuated(dve, ("S", s, i2))
                                nc.vector.tensor_tensor(sink_e[:, heads], sink[:, heads], neg_max[:, heads],
                                                        ALU.add).then_inc(sink_in_ready, 1)
                                dve.wait_ge(sink_e_ready, 2 * t + i + 1)
                                dve.wait_ge(probs_ready, HEADS * s + j + 1)
                                link(nc.vector.tensor_tensor(row_sum[:, heads], row_sum[:, heads], sink_e[:, heads], ALU.add))
                            dve.wait_ge(probs_ready, HEADS * s + j + 1)
                            link(nc.vector.reciprocal(row_sum[:, heads], row_sum[:, heads]))
                elif piece == "out":
                    for i in range(2):
                        dve.wait_ge(pv_done, HEADS * s + 8 * (i + 1))
                        heads = slice(8 * i, 8 * i + 8)
                        o = attended[:, CW * i:CW * i + CW].rearrange("p (h d) -> p h d", d=HD)
                        ins = nc.vector.tensor_tensor(
                            o, o_banks[i][:, :].rearrange("p (h d) -> p h d", d=HD),
                            row_sum[:, heads].unsqueeze(2).to_broadcast([P, 8, HD]), ALU.mult)
                        ins.then_inc(o_free, 1)
                    if l == 0:
                        dve.wait_ge(o_free, 2 * s + 2)
                        nc.vector.tensor_tensor(attended[:, CW:2 * CW], attended[:, CW:2 * CW], gate[:, t, :],
                                                ALU.mult).then_inc(gated, 1)
                    for c in range(2):
                        use = ("out", s, c)
                        mm.wait_full(dve, use)
                        xc = x[:, t, CW * c:CW * c + CW]
                        nc.vector.tensor_tensor(xc, xc, mm.bank(use)[:, :], ALU.add).then_inc(mm.freed(use), 1)
                elif piece == "ffn":
                    dve.wait_ge(rms2_ready, s + 1)
                    dve.wait_ge(norms_in, 16 * (l + 1))
                    norm(x[:, t, :], gain_ffn, h_ffn[:, s % 2, :]).then_inc(h2_ready, 1)
                elif piece.startswith("topk"):
                    b = int(piece[4])
                    use = ("sc", s, b)
                    mm.wait_full(dve, use)
                    for i in range(4):
                        last = top16(mm.bank(use)[:, i * NK:(i + 1) * NK], top_v[:, i, :], top_i[:, i, :], rest[:, 0:NK])
                        if i < 3:
                            tick(last)
                    last.then_inc(mm.freed(use), 1)
                    mm.wait_evacuated(dve, use)
                    for h in range(2):
                        link(nc.vector.tensor_tensor(
                            cand[:, :].rearrange("p (a b) -> p a b", a=TK),
                            top_v[:, 2 * h, :].unsqueeze(2).to_broadcast([P, TK, TK]),
                            top_v[:, 2 * h + 1, :].unsqueeze(1).to_broadcast([P, TK, TK]), ALU.add))
                        tick(top16(cand[:, :], best_v[:, 2 * b + h, :], best_i[:, h, :], rest[:, :]))
                    tick(nc.vector.tensor_copy(top_if[:, :, :], top_i[:, :, :]))
                    settle()
                    pair = best_v[:, 2 * b:2 * b + 2, :]
                    link(nc.vector.tensor_copy(g_sum[:, :].unsqueeze(2), pair[:, :, 0:1]))
                    nc.vector.tensor_tensor(pair, pair, g_sum[:, :].unsqueeze(2).to_broadcast([P, 2, TK]),
                                            ALU.subtract).then_inc(best_ready, 1)
                    flat_i = best_i[:, :, :].rearrange("p a b -> p (a b)")
                    oh3 = onehot.rearrange("p (a b) -> p a b", b=TK)
                    oh4 = onehot.rearrange("p (h a b) -> p h a b", h=2, b=TK)
                    for half, (dst, op, by) in enumerate(((id_1, ALU.logical_shift_right, 4), (id_2, ALU.bitwise_and, 15))):
                        link(nc.vector.tensor_single_scalar(half_i[:, :], flat_i, by, op))
                        link(nc.vector.tensor_copy(half_f[:, :], half_i[:, :]))
                        link(nc.vector.tensor_tensor(oh3, half_f[:, :].unsqueeze(2).to_broadcast([P, 2 * TK, TK]),
                                                     iota.unsqueeze(1).to_broadcast([P, 2 * TK, TK]), ALU.is_equal))
                        names = top_if[:, :, :].rearrange("p (h two) b -> p h two b", two=2)[:, :, half, :]
                        link(nc.vector.tensor_tensor(oh4, oh4, names.unsqueeze(2).to_broadcast([P, 2, TK, TK]), ALU.mult))
                        link(nc.vector.tensor_reduce(dst[:, :], oh3, AX_X, ALU.add))
                    link(nc.vector.tensor_scalar(id_1[:, :], id_1[:, :], float(NK), float(l * EXPERTS), ALU.mult, ALU.add))
                    link(nc.vector.tensor_tensor(id_1[:, :], id_1[:, :], id_2[:, :], ALU.add))
                    at = PH * TK * s + 2 * TK * b
                    nc.vector.tensor_copy(ids[:, at:at + 2 * TK], id_1[:, :]).then_inc(ids_ready, 2)
                    dve.wait_ge(gexp_ready, 4 * s + b + 1)
                    link(nc.vector.tensor_reduce(g_sum[:, :], pair, AX_X, ALU.add))
                    link(nc.vector.reciprocal(g_sum[:, :], g_sum[:, :]))
                    link(nc.vector.tensor_tensor(
                        gates[:, at:at + 2 * TK].rearrange("p (a b) -> p a b", a=2), pair,
                        g_sum[:, :].unsqueeze(2).to_broadcast([P, 2, TK]), ALU.mult))

            def unit(u, s):
                for k in range(RING):
                    dve.wait_ge(down_in[k], 16 * (u + 1))
                    nc.vector.scalar_tensor_tensor(
                        down_rows[:, k, :], down_rows[:, k, :], 1.0, h_ffn[:, s % 2, :], ALU.mult, ALU.mult,
                        accum_out=dots[:, k:k + 1]).then_inc(dots_done, 1)
                dve.wait_ge(gelu_done, u + 1)
                now = gates[:, bass.ds(RING * u, RING)]
                nc.vector.tensor_tensor(now, gelus[:, :], now, ALU.mult).then_inc(w_ready, 1)

            dve.wait_ge(consts_in, 16)
            for step in SCHEDULE:
                if step[0] == "front":
                    front(*step[1:])
                elif step[0] == "chunks":
                    for c in step[2]:
                        projection(("proj", step[1], c))
                elif step[0] == "first dots":
                    for u in range(AHEAD):
                        unit(u, 0)
                elif step[0] == "units":
                    s, a, b = step[1:]
                    a, b = UNITS * s + a + AHEAD, UNITS * s + b + AHEAD
                    if b - a > 1:
                        with dve.Fori(a, b) as u:
                            unit(u, s)
                    else:
                        unit(a, s)
                elif step[0] == "close" and step[1] < 3:
                    for u in range(AHEAD):
                        unit(UNITS * (step[1] + 1) + u, step[1] + 1)


def kernel(x, attn_norm, ffn_norm, ev_w_in, ev_forget_bias, ev_q_norm_a, ev_k_norm_a,
           ev_q_norm_b, ev_k_norm_b, ev_w_out, od_w_in, od_q_norm, od_k_norm, od_sinks,
           od_w_out, peer_w_query, peer_sub_keys, peer_down, peer_up):
    import numpy as np
    import concourse.bacc as bacc
    from concourse.bass_utils import run_bass_kernel_spmd

    seq = np.arange(2 * P, dtype=np.float32)
    inv_freq = np.power(np.float32(500000.0), -np.arange(0, 2 * ROT, 2, dtype=np.float32) / np.float32(2 * ROT))
    ang = (seq[:, None] * inv_freq[None, :]).astype(np.float32)
    c = np.zeros((P, C_END), np.float32)
    i, j = np.arange(P)[:, None], np.arange(P)[None, :]
    c[:, C_ID:C_ID + P] = i == j
    c[:, C_M0 + P:C_M0 + 2 * P] = np.where(j <= i, 0.0, NEG_INF)
    c[:, C_M1 + P:C_M1 + 2 * P] = np.where(j <= i, 0.0, NEG_INF)
    c[:, C_M1:C_M1 + P] = np.where(j > i, 0.0, NEG_INF)
    c[:, C_TRI:C_TRI + P] = i <= j
    c[:, C_ONES:C_ONES + P] = 1.0
    for t in range(2):
        c[:, C_COS + ROT * t:C_COS + ROT * (t + 1)] = np.cos(ang[P * t:P * (t + 1)])
        c[:, C_SIN + ROT * t:C_SIN + ROT * (t + 1)] = np.sin(ang[P * t:P * (t + 1)])
    c[:, C_IOTA:C_IOTA + TK] = np.arange(TK)
    c[:, C_EPS] = EPS
    con = np.ascontiguousarray
    a = np.asarray
    arrays = {
        "x_in": con(a(x)[0]), "consts": c, "attn_norm": con(a(attn_norm)), "ffn_norm": con(a(ffn_norm)),
        "w_in0": con(a(ev_w_in)[0]), "fbias": con(a(ev_forget_bias)[0]),
        "head_gains0": np.stack([a(ev_q_norm_a)[0], a(ev_k_norm_a)[0], a(ev_q_norm_b)[0], a(ev_k_norm_b)[0]]),
        "w_out0": con(a(ev_w_out)[0]), "w_in1": con(a(od_w_in)[0]),
        "head_gains1": np.stack([a(od_q_norm)[0], a(od_k_norm)[0]]), "sinks": con(a(od_sinks)[0]),
        "w_out1": con(a(od_w_out)[0]), "w_query": con(a(peer_w_query)),
        "keys_t": con(a(peer_sub_keys).transpose(4, 0, 1, 2, 3).reshape(HD, 2, 2 * PH, NK)),
        "down": con(a(peer_down).reshape(2 * EXPERTS, D)), "up": con(a(peer_up).reshape(2 * EXPERTS, D)),
    }
    nc = bacc.Bacc("TRN2", target_bir_lowering=False, num_devices=1)
    args = [nc.dram_tensor(k, v.shape, mybir.dt.from_np(v.dtype), kind="ExternalInput").ap() for k, v in arrays.items()]
    args.append(nc.dram_tensor("out", (2 * P, D), F32, kind="ExternalOutput").ap())
    build(nc, *args)
    r = run_bass_kernel_spmd(nc, [arrays], core_ids=[0])
    return r.results[0]["out"].reshape(1, 2 * P, D)
```

```python
from contextlib import ExitStack

import concourse.bass as bass
from concourse import mybir

ALU = mybir.AluOpType
ACT = mybir.ActivationFunctionType
F32 = mybir.dt.float32
U32 = mybir.dt.uint32
AX_X = mybir.AxisListType.X

P = 128
D = 1024
KT = D // P
HD = 64
HEADS = 16
EPS = 1e-6
NEG_INF = -1e30
BIG = 3.0e38
SCALE = HD ** -0.5
ROT = 8
CW = 512
PH = 8
TK = 16
NK = 128
EXPERTS = NK * NK
STAGES = [(0, 0), (0, 1), (1, 0), (1, 1)]
RING = 8
DIAGS = RING
WSLOTS = 2
AUGW = HD + 2

C_ID, C_M0, C_TRI, C_ONES, C_M1, C_COS, C_SIN, C_IOTA, C_EPS, C_END = 0, 128, 384, 512, 640, 896, 912, 928, 944, 945

CHUNKS = [[(CW * c, CW) for c in range(7)] + [(7 * CW, 8)], [(0, CW), (CW, CW), (2 * CW, 256)]]
UNITS = PH * TK // RING
AHEAD = 2
PIECE_CHUNKS = {"proj0": (0,), "proj1": (1,), "proj2": (2,)}
REST = ("wq rest", 0, 0)
SIDE = [("proj", 1, 6), ("proj", 1, 2), ("proj", 1, 5), REST, ("proj", 1, 0), ("proj", 1, 4)]
EARLY = [("proj", 1, c) for c in (5, 0, 4)]


def schedule():
    steps = [("front", 0, "norm"), ("front", 0, "turn"), ("chunks", 0, (7, 0)), ("front", 1, "norm"),
             ("chunks", 0, (1,)), ("front", 1, "turn"), ("front", 0, "forget"), ("chunks", 0, (3,)),
             ("front", 0, "decay"), ("chunks", 0, (4, 2)), ("front", 0, "heads"), ("chunks", 0, (6,)),
             ("front", 0, "gate"), ("chunks", 0, (5,))]
    steps += [("front", 0, "attn"), ("front", 0, "out"), ("multiply", SIDE[2]), ("front", 0, "ffn"),
              ("front", 0, "wq0"), ("collect", SIDE[2]), ("front", 0, "wq1")]
    steps += [("front", 0, p) for p in ("topk0", "topk1", "gates0", "gates1")]
    steps += [("dots", 0), ("dots", 1), ("chunks", 1, (0, 4, 1, 3, 7))]
    for s in range(4):
        steps.append(("open", s))
        if s == 0:
            own = ["topk2", "topk3 gates2", "topk4 gates3", "topk5 gates4", "topk6 gates5", "topk7 gates6", "gates7"]
            new = ["", "", "forget", "gate", "decay heads", "attn0", "attn1", "attn2 attn3", "out", "ffn wq0"]
        else:
            own = ["topk5 gates4", "topk6 gates5", "topk7 gates6", "gates7"]
            new = ["norm", "turn proj0", "proj1", "proj2", "heads attn0", "attn1", "attn2 attn3", "out", "", "ffn wq0"]
        new += ["topk0", "topk1 gates0", "wq1 topk2 gates1", "topk3 gates2", "topk4 gates3"]
        pieces = [[(s, p) for p in ps.split()] for ps in own] + [[] for _ in new[len(own):]]
        if s < 3:
            for at, ps in enumerate(new):
                ahead = [(s + 1, p) for p in ps.split() if p in ("norm", "forget", "decay", "heads")]
                pieces[at] = ahead + pieces[at] + [(s + 1, p) for p in ps.split() if (s + 1, p) not in ahead]
        steps += [("front", f, p) for f, p in pieces.pop(0)]
        while not pieces[-1]:
            pieces.pop()
        at = 0
        for end, ps in enumerate(pieces, 1):
            if not ps:
                continue
            steps.append(("units", s, at, end))
            steps += [("front", f, p) for f, p in ps]
            at = end
        steps += [("units", s, at, UNITS - AHEAD)] * (at < UNITS - AHEAD) + [("close", s)]
    return steps


def companion(s, j):
    return (SIDE[j // KT], j % KT) if s == 0 else (None, None)


def next_scores(s, piece):
    return ({"topk0": 1, "topk3": 2, "topk4": 3} if s else {"topk2": 2, "topk4": 3}).get(piece)


def attn_heads(piece):
    return (0, HEADS) if piece == "attn" else (4 * int(piece[4]), 4 * int(piece[4]) + 4)


def head_span(l, c):
    if l == 0:
        return {0: (0, 8, 0), 1: (8, 8, 1), 3: (16, 8, 2), 4: (24, 8, 3)}.get(c)
    return ((0, 8, 0), (8, 8, 0), (16, 2, 1))[c]


def bank_uses():
    mm, tp, chunks = [], [], []

    def take(*uses):
        for use in uses:
            chunks.append(use)
            if use not in SIDE:
                mm.append(use)

    for step in SCHEDULE:
        if step[0] == "chunks":
            take(*[("proj", step[1], c) for c in step[2]])
        if step[0] == "multiply":
            take(step[1])
        if step[0] == "open" and step[1] == 0:
            mm.append(("sc", 0, 1))
        if step[0] != "front":
            continue
        _, s, piece = step
        l = STAGES[s][0]
        if piece == "turn":
            tp += [("h1", s, i) for i in range(2)]
        elif piece in PIECE_CHUNKS:
            take(*[("proj", s, c) for c in PIECE_CHUNKS[piece]])
        elif piece == "decay":
            mm.append(("F", s))
        elif piece == "heads":
            tp += [("qk", s, g) for g in range(8 if l == 0 else 5)]
        elif piece.startswith("attn"):
            first, end = attn_heads(piece)
            mm += [("S", s, j) for j in range(first, end)]
            tp += [("PT", s, j) for j in range(first, end)]
            if s == 0:
                take(*SIDE[0:2])
        elif piece == "out":
            tp += [("att", s, i) for i in range(2)]
            take(*[("out", s, c) for c in range(2)])
        elif piece == "ffn":
            tp += [("h2", s, i) for i in range(2)]
        elif piece in ("wq0", "wq1"):
            c = int(piece[2])
            take(("wq", s, c))
            tp += [("pq", s, g) for g in (2 * c, 2 * c + 1)]
            mm += [("sc", s, 0)] * (c == 0)
        elif next_scores(s, piece):
            mm.append(("sc", s, next_scores(s, piece)))
    return mm, tp, chunks


def chunk_places(chunks):
    places, first, rest = {}, 0, 0
    for use in chunks:
        if use in EARLY:
            places[use] = 4 + EARLY.index(use) % 2
        elif use[1] == 0 or use in SIDE:
            places[use] = first % 4
            first += 1
        else:
            places[use] = 2 + rest % 2
            rest += 1
    return places


SCHEDULE = schedule()


def q_head(layer, j):
    return j if layer == 1 or j < 8 else 16 + j - 8


def k_head(layer, j):
    return 16 + j // 8 if layer == 1 else 8 + j if j < 8 else 24 + j - 8


def k_rows(layer, j):
    return HD if layer == 1 or j < 8 else AUGW


class Banks:

    def __init__(self, full, free, tensors, uses):
        self.full, self.free, self.tensors = full, free, tensors
        self.number = {u: n for n, u in enumerate(uses)}

    def bank(self, use):
        return self.tensors[self.number[use] % 2]

    def freed(self, use):
        return self.free[self.number[use] % 2]

    def wait_room(self, eng, use):
        n = self.number[use]
        if n >= 2:
            eng.wait_ge(self.free[n % 2], n // 2)

    def wait_full(self, eng, use):
        eng.wait_ge(self.full, self.number[use] + 1)

    def wait_evacuated(self, eng, use):
        n = self.number[use]
        eng.wait_ge(self.free[n % 2], n // 2 + 1)


def build(nc, x_in, consts, attn_norm, ffn_norm, w_in0, fbias, head_gains0, w_out0, w_in1,
          head_gains1, sinks, w_out1, w_query, keys_t, down, up, out):
    ctx = ExitStack()
    with ctx:
        def sb(name, shape, dt=F32):
            return ctx.enter_context(nc.sbuf_tensor(name, shape, dt))

        def sem(name):
            return ctx.enter_context(nc.semaphore(name))

        cst = sb("cst", [P, C_END])
        ident = cst[:, C_ID:C_ID + P]
        masks = [cst[:, C_M0:C_M0 + 2 * P], cst[:, C_M1:C_M1 + 2 * P]]
        tri = cst[:, C_TRI:C_TRI + P]
        ones = cst[:, C_ONES:C_ONES + P]
        iota = cst[:, C_IOTA:C_IOTA + TK]
        eps = cst[:, C_EPS:C_EPS + 1]
        down_rows = sb("down_rows", [P, RING, D])
        up_rows = sb("up_rows", [P, RING, D])
        diags = sb("diags", [P, DIAGS, P])
        x = sb("x", [P, 2, D])
        h_ffn = sb("h_ffn", [P, 2, D])
        gain_attn = sb("gain_attn", [P, D])
        gain_ffn = sb("gain_ffn", [P, D])
        act_t = sb("act_t", [P, KT, P])
        weights = sb("weights", [P, WSLOTS, KT, CW])
        keys = sb("keys", [HD, 2 * PH, NK])
        raw = sb("raw", [P, 2 * D])
        squares = raw[:, 0:CW].rearrange("p (h d) -> p h d", d=HD)
        h_attn = raw[:, D:2 * D]
        h1_t = [h_ffn[:, 1, :].rearrange("p (a b) -> p a b", a=KT) if s == 1 else act_t for s in range(4)]
        attended = raw[:, 0:D]
        queries = raw[:, D:2 * D]
        aug = sb("aug", [P, 32, AUGW])
        q_t = sb("q_t", [AUGW, HEADS, P])
        k_t = sb("k_t", [AUGW, HEADS, 2 * P])
        v = sb("v", [P, 2, D])
        gate = sb("gate", [P, 2, CW])
        probs = sb("probs", [P, 2, 2 * P])
        onehot = probs[:, :, :].rearrange("p h (a b) -> p h a b", a=TK)
        probs_t = sb("probs_t", [P, 2, 2 * P])
        ids = sb("ids", [P, 4 * PH * TK], U32)
        gates = sb("gates", [P, 4 * PH * TK])
        down_ids = sb("down_ids", [P, 2, RING], U32)
        up_ids = sb("up_ids", [P, 2, RING], U32)
        dots = sb("dots", [P, RING])
        gelus = sb("gelus", [P, RING])
        w_now = sb("w_now", [P, RING])
        g_heads = [sb("g_heads0", [P, 4, HD]), sb("g_heads1", [P, 2, HD])]
        sink = sb("sink", [P, HEADS])
        f_bias = sb("f_bias", [P, 8])
        sumsq = sb("sumsq", [P, 1])
        rms = sb("rms", [P, 1])
        rstd = sb("rstd", [P, 1])
        head_ss = sb("head_ss", [P, 8])
        rope_tmp = raw[:, 0:4 * 18 * ROT].rearrange("p (a h r) -> p a h r", a=4, h=18)
        fz = sb("fz", [P, 2, 4, 8])
        log_f = sb("log_f", [P, 2, 8])
        neg_max = sb("neg_max", [P, HEADS])
        row_sum = sb("row_sum", [P, HEADS])
        sink_e = sb("sink_e", [P, HEADS])
        neg_sink = sb("neg_sink", [P, HEADS])
        top_v = sb("top_v", [P, 2, TK])
        top_i = sb("top_i", [P, 2, TK], U32)
        rest = sb("rest", [P, TK * TK])
        cand = sb("cand", [P, TK * TK])
        best_v = sb("best_v", [P, 2, TK])
        neg_best = sb("neg_best", [P, 2])
        best_i = sb("best_i", [P, TK], U32)
        top_if = sb("top_if", [P, 2, TK])
        half_i = sb("half_i", [P, 2, TK], U32)
        half_f = sb("half_f", [P, 2, TK])
        chosen = sb("chosen", [P, 2, TK])
        id_f = sb("id_f", [P, TK])
        g_sum = sb("g_sum", [P, 2])

        def bank(name):
            return ctx.enter_context(nc.psum_tensor(name, [P, CW], F32))

        acc = [bank("acc0"), bank("acc1")]
        mm_banks = [bank("mm0"), bank("mm1")]
        tp_banks = [bank("tp0"), bank("tp1")]
        o_banks = [bank("o0"), bank("o1")]

        consts_in = sem("consts_in")
        x_in_sem = [sem("x_in0"), sem("x_in1")]
        attn_gain_in = sem("attn_gain_in")
        norms_in = sem("norms_in")
        small_in = sem("small_in")
        keys_in = sem("keys_in")
        weights_in = [sem(f"weights_in{i}") for i in range(6)]
        mm_full, mm_free = sem("mm_full"), [sem("mm_free0"), sem("mm_free1")]
        side_full, side_free = sem("side_full"), [sem("side_free0"), sem("side_free1")]
        tp_full, tp_free = sem("tp_full"), [sem("tp_free0"), sem("tp_free1")]
        dve_step = sem("dve_step")
        ss1_ready, rms1_ready, h1_ready = sem("ss1_ready"), sem("rms1_ready"), sem("h1_ready")
        rms2_ready, head_ss_ready, head_rms_ready = sem("rms2_ready"), sem("head_ss_ready"), sem("head_rms_ready")
        squares_ready, aug_ready = sem("squares_ready"), sem("aug_ready")
        fz_ready, fe_ready, fln_ready = sem("fz_ready"), sem("fe_ready"), sem("fln_ready")
        log_f_ready, f_ready = sem("log_f_ready"), sem("f_ready")
        probs_ready = sem("probs_ready")
        pv_done, o_free = sem("pv_done"), sem("o_free")
        sink_in_ready, sink_e_ready = sem("sink_in_ready"), sem("sink_e_ready")
        gated = sem("gated")
        ss2_ready, h2_ready = sem("ss2_ready"), sem("h2_ready")
        best_ready, gexp_ready, ids_ready = sem("best_ready"), sem("gexp_ready"), sem("ids_ready")
        down_in = [sem(f"down_in{i}") for i in range(RING)]
        up_in = [sem(f"up_in{i}") for i in range(RING)]
        down_staged, up_staged = sem("down_staged"), sem("up_staged")
        slots_claimed = sem("slots_claimed")
        dots_done, gelu_done = sem("dots_done"), sem("gelu_done")
        w_ready, w_taken = sem("w_ready"), sem("w_taken")
        diag_ready, up_done = sem("diag_ready"), sem("up_done")
        x_out_ready, out_written = sem("x_out_ready"), sem("out_written")

        mm_uses, tp_uses, chunk_list = bank_uses()
        head_chunks = [u for u in chunk_list if u[0] == "proj" and head_span(STAGES[u[1]][0], u[2])]
        norm_no = {u: n for n, u in enumerate(head_chunks)}
        mm = Banks(mm_full, mm_free, mm_banks, mm_uses)
        tp = Banks(tp_full, tp_free, tp_banks, tp_uses)
        side = Banks(side_full, side_free, acc, SIDE)
        place = chunk_places(chunk_list)
        same_place = {u: [w for w in chunk_list if place[w] == place[u]] for u in chunk_list}
        halves = [rows[:, 4 * i:4 * i + 4, :].rearrange("p k (b n) -> p (k b) n", n=CW)
                  for rows in (down_rows, up_rows) for i in range(2)]
        chunk_at = halves[0:2] + [weights[:, 0], weights[:, 1]] + halves[2:4]

        def banks_of(use):
            return side if use in SIDE else mm

        def chunk_cols(use):
            kind, s, c = use
            return CHUNKS[STAGES[s][0]][c] if kind == "proj" else (CW * c, CW)

        def columns(use):
            if use == REST:
                return CW // 2, CW
            return (0, CW // 2) if use == ("wq", 0, 0) else (0, chunk_cols(use)[1])

        def chunk_source(use):
            kind, s, c = use
            l = STAGES[s][0]
            a, w = chunk_cols(use)
            m = {"proj": (w_in0, w_in1), "out": (w_out0, w_out1), "wq": (w_query[0], w_query[1])}[kind][l]
            return m[:, a:a + w].rearrange("(kt p) n -> p kt n", p=P)

        def qk_group(s, g):
            l = STAGES[s][0]
            if g < 4:
                return [(q_head(l, j), j, k_rows(l, j)) for j in range(4 * g, 4 * g + 4)]
            if l == 0:
                return [(k_head(l, j), j, k_rows(l, j)) for j in range(4 * (g - 4), 4 * (g - 4) + 4)]
            return [(16 + i, i, HD) for i in range(2)]

        def v_cols(l, j):
            return slice(HD * j, HD * j + HD) if l == 0 else slice(HD * (j // 8), HD * (j // 8) + HD)

        def wait_residual(eng, s):
            for c in range(2):
                mm.wait_evacuated(eng, ("out", s, c))

        block = ctx.enter_context(nc.Block())

        @block.sync
        def _(sp):
            def layer_loads(l):
                sp.dma_start(gain_ffn[:, :], ffn_norm[l].partition_broadcast(P)).then_inc(norms_in, 16)
                sp.dma_start(keys[:, :, :], keys_t[:, l]).then_inc(keys_in, 16)

            def gain_load(l):
                sp.dma_start(gain_attn[:, :], attn_norm[l].partition_broadcast(P)).then_inc(attn_gain_in, 16)

            sp.dma_start(x[:, 0, :], x_in[0:P, :]).then_inc(x_in_sem[0], 16)
            gain_load(0)
            late = chunk_list.index(EARLY[-1])
            order = chunk_list[:late] + chunk_list[late + 1:late + 3] + [EARLY[-1]] + chunk_list[late + 3:]
            for use in order:
                if use == ("proj", 2, 0):
                    sp.wait_ge(h2_ready, 2)
                    mm.wait_full(sp, ("sc", 1, 3))
                    gain_load(1)
                    layer_loads(1)
                number = same_place[use].index(use)
                if number:
                    last = same_place[use][number - 1]
                    banks_of(last).wait_full(sp, last)
                w = chunk_cols(use)[1]
                sp.dma_start(chunk_at[place[use]][:, :, 0:w], chunk_source(use)).then_inc(weights_in[place[use]], 16)
                if use == ("proj", 0, 0):
                    sp.dma_start(x[:, 1, :], x_in[P:2 * P, :]).then_inc(x_in_sem[1], 16)
                if use == SIDE[1]:
                    layer_loads(0)
            for t in range(2):
                sp.wait_ge(x_out_ready, 2 * (2 + t) + 2)
                sp.dma_start(out[t * P:(t + 1) * P, :], x[:, t, :]).then_inc(out_written, 16)
            sp.wait_ge(out_written, 32)

        @block.gpsimd
        def _(pool):
            def gather(table, rows, id_column, k, landed):
                pool.indirect_dma_start(
                    out=rows[:, k, :], out_offset=None, in_=table,
                    in_offset=bass.IndirectOffsetOnAxis(ap=id_column, axis=0)).then_inc(landed[k], 16)

            def slot(n, k, parity, table, rows, ids_now, staged, used, landed):
                if not (isinstance(n, int) and n <= 0):
                    pool.wait_ge(used, RING * n + k + 1 - RING)
                    pool.sem_inc(slots_claimed, 1)
                if k == 0:
                    nc.gpsimd.tensor_copy(ids_now[:, parity, :], ids[:, bass.ds(RING * n, RING)]).then_inc(staged, 1)
                    pool.wait_ge(staged, n + 1)
                    pool.sem_inc(slots_claimed, 1)
                gather(table, rows, ids_now[:, parity, k:k + 1], k, landed)

            def down_slot(n, k, parity):
                slot(n, k, parity, down, down_rows, down_ids, down_staged, dots_done, down_in)

            def up_slot(n, k, parity):
                slot(n, k, parity, up, up_rows, up_ids, up_staged, up_done, up_in)

            def head(g, last=False):
                if not last:
                    pool.wait_ge(ids_ready, g + 2)
                for half in range(2):
                    n = 2 * g + half
                    for k in range(RING):
                        if not last:
                            down_slot(n + AHEAD, k, half)
                        up_slot(n, k, half)

            pool.wait_ge(ids_ready, 1)
            side.wait_full(pool, REST)
            for n in range(AHEAD):
                for k in range(RING):
                    if n == 0 and k == RING // 2:
                        mm.wait_full(pool, ("wq", 0, 1))
                    down_slot(n, k, n)
            side.wait_full(pool, EARLY[-1])
            head(0)
            with pool.Fori(1, 4 * PH - 1) as g:
                head(g)
            head(4 * PH - 1, last=True)

        @block.scalar
        def _(act):
            def evacuate(banks, use, dst, src):
                banks.wait_full(act, use)
                nc.scalar.copy(dst, src).then_inc(banks.freed(use), 1)

            def transposed(kind, s, dst=act_t):
                for i in range(2):
                    evacuate(tp, (kind, s, i), dst[:, 4 * i:4 * i + 4, :],
                             tp.bank((kind, s, i))[:, :].rearrange("p (a b) -> p a b", a=4))

            def projection(use):
                _, s, c = use
                l, t = STAGES[s]
                banks = banks_of(use)
                b = banks.bank(use)
                heads_of = b[:, :].rearrange("p (h d) -> p h d", d=HD)
                if l == 1 and c == 2:
                    banks.wait_full(act, use)
                    nc.scalar.copy(v[:, t, 0:P], b[:, P:2 * P])
                    evacuate(banks, use, aug[:, 16:18, 0:HD], heads_of[:, 0:2, :])
                elif head_span(l, c):
                    a, n, _ = head_span(l, c)
                    evacuate(banks, use, aug[:, a:a + n, 0:HD], heads_of)
                elif c in (2, 5):
                    i = c // 5
                    evacuate(banks, use, v[:, t, CW * i:CW * i + CW], b[:, :])
                elif c == 6:
                    banks.wait_full(act, use)
                    nc.scalar.activation(gate[:, t, :], b[:, :], ACT.Exp, scale=-1.0).then_inc(banks.freed(use), 1)
                if head_span(l, c):
                    a, n, _ = head_span(l, c)
                    banks.wait_evacuated(act, use)
                    nc.scalar.activation(squares[:, 0:n, :], aug[:, a:a + n, 0:HD], ACT.Square).then_inc(squares_ready, 1)
                    act.wait_ge(head_ss_ready, norm_no[use] + 1)
                    nc.scalar.activation(head_ss[:, 0:n], head_ss[:, 0:n], ACT.Sqrt, scale=1.0 / HD,
                                         bias=eps).then_inc(head_rms_ready, 1)

            def front(s, piece):
                l, t = STAGES[s]
                nkeys = (t + 1) * P
                if piece == "norm":
                    if l == 0:
                        act.wait_ge(x_in_sem[t], 16)
                    else:
                        act.wait_ge(x_out_ready, 2 * (s - 2) + 2)
                    if s == 1:
                        tp.wait_full(act, ("h1", 0, 1))
                    elif s:
                        tp.wait_full(act, ("pq", s - 1, 3))
                    nc.scalar.activation(h_attn, x[:, t, :], ACT.Square, accum_out=sumsq[:, :]).then_inc(ss1_ready, 1)
                    act.wait_ge(ss1_ready, s + 1)
                    nc.scalar.activation(rms[:, :], sumsq[:, :], ACT.Sqrt, scale=1.0 / D, bias=eps).then_inc(rms1_ready, 1)
                elif piece == "turn":
                    if s >= 2:
                        mm.wait_full(act, ("wq", s - 1, 1))
                    transposed("h1", s, h1_t[s])
                elif piece in PIECE_CHUNKS:
                    for c in PIECE_CHUNKS[piece]:
                        projection(("proj", s, c))
                elif piece == "forget":
                    act.wait_ge(fz_ready, s + 1)
                    nc.scalar.activation(fz[:, t, 2, :], fz[:, t, 1, :], ACT.Exp).then_inc(fe_ready, 1)
                    act.wait_ge(fe_ready, s + 1)
                    nc.scalar.activation(fz[:, t, 3, :], fz[:, t, 2, :], ACT.Ln, bias=1.0).then_inc(fln_ready, 1)
                elif piece == "heads":
                    if s:
                        mm.wait_full(act, ("sc", s - 1, 3))
                    for g in range(8 if l == 0 else 5):
                        heads = qk_group(s, g)
                        use = ("qk", s, g)
                        n, rows = len(heads), heads[0][2]
                        j = heads[0][1]
                        src = tp.bank(use)[0:rows, 0:n * P].rearrange("p (a b) -> p a b", a=n)
                        dst = q_t[0:rows, j:j + n, :] if g < 4 else k_t[0:rows, j:j + n, t * P:(t + 1) * P]
                        evacuate(tp, use, dst, src)
                elif piece.startswith("attn"):
                    first, end = attn_heads(piece)

                    def transposed_probs(j):
                        if j >= 2 or s:
                            act.wait_ge(pv_done, HEADS * s + j - 1)
                        evacuate(tp, ("PT", s, j), probs_t[:, j % 2, 0:nkeys], tp.bank(("PT", s, j))[:, 0:nkeys])
                        use, k = companion(s, j)
                        if k == KT - 1:
                            projection(use)

                    for j in range(first, end):
                        mm.wait_evacuated(act, ("S", s, j))
                        nc.scalar.activation(probs[:, j % 2, 0:nkeys], probs[:, j % 2, 0:nkeys], ACT.Exp,
                                             scale=-1.0, bias=neg_max[:, j:j + 1],
                                             accum_out=row_sum[:, j:j + 1]).then_inc(probs_ready, 1)
                        if j > first:
                            transposed_probs(j - 1)
                        if l == 1 and j % 8 == 7:
                            i = j // 8
                            act.wait_ge(sink_in_ready, 2 * t + i + 1)
                            nc.scalar.activation(sink_e[:, 8 * i:8 * i + 8], sink_e[:, 8 * i:8 * i + 8],
                                                 ACT.Exp).then_inc(sink_e_ready, 1)
                    transposed_probs(end - 1)
                elif piece == "out":
                    mm.wait_full(act, ("proj", s, (5, 7, 2, 2)[s]))
                    transposed("att", s)
                elif piece == "ffn":
                    wait_residual(act, s)
                    nc.scalar.activation(queries, x[:, t, :], ACT.Square, accum_out=sumsq[:, :]).then_inc(ss2_ready, 1)
                    act.wait_ge(ss2_ready, s + 1)
                    nc.scalar.activation(rms[:, :], sumsq[:, :], ACT.Sqrt, scale=1.0 / D, bias=eps).then_inc(rms2_ready, 1)
                    mm.wait_full(act, ("out", s, 1))
                    transposed("h2", s)
                elif piece in ("wq0", "wq1"):
                    c = int(piece[2])
                    w = columns(("wq", s, c))[1]
                    evacuate(mm, ("wq", s, c), queries[:, CW * c:CW * c + w], mm.bank(("wq", s, c))[:, 0:w])
                    for g in (2 * c, 2 * c + 1):
                        if (s, g) == (0, 1):
                            evacuate(side, REST, queries[:, CW // 2:CW], side.bank(REST)[:, 0:CW // 2])
                        evacuate(tp, ("pq", s, g), q_t[0:HD, 4 * g:4 * g + 4, :],
                                 tp.bank(("pq", s, g))[0:HD, :].rearrange("p (a b) -> p a b", a=4))
                elif piece.startswith("gates"):
                    h = int(piece[5])
                    act.wait_ge(best_ready, PH * s + h + 1)
                    nc.scalar.activation(best_v[:, h % 2, :], best_v[:, h % 2, :], ACT.Exp, bias=neg_best[:, h % 2:h % 2 + 1],
                                         accum_out=g_sum[:, h % 2:h % 2 + 1]).then_inc(gexp_ready, 1)

            def gelu(u):
                act.wait_ge(dots_done, RING * (u + 1))
                nc.scalar.activation(gelus[:, :], dots[:, :], ACT.Gelu).then_inc(gelu_done, 1)

            def unit(u, with_down=True):
                act.wait_ge(w_ready, u + 1)
                if not (isinstance(u, int) and u == 0):
                    act.wait_ge(diag_ready, RING * u)
                nc.scalar.copy(w_now[:, :], gates[:, bass.ds(RING * u, RING)]).then_inc(w_taken, 1)
                act.wait_ge(w_taken, u + 1)
                for k in range(RING):
                    if not (isinstance(u, int) and RING * u + k + 1 - DIAGS <= 0):
                        act.wait_ge(up_done, RING * u + k + 1 - DIAGS)
                    nc.scalar.activation(diags[:, k, :], ident, ACT.Copy, scale=w_now[:, k:k + 1]).then_inc(diag_ready, 1)
                if with_down:
                    gelu(u + AHEAD)

            act.dma_start(cst[:, :], consts).then_inc(consts_in, 16)
            act.dma_start(g_heads[0][:, :, :], head_gains0.partition_broadcast(P)).then_inc(small_in, 16)
            act.dma_start(g_heads[1][:, :, :], head_gains1.partition_broadcast(P)).then_inc(small_in, 16)
            act.dma_start(sink[:, :], sinks.partition_broadcast(P)).then_inc(small_in, 16)
            act.dma_start(f_bias[:, :], fbias.partition_broadcast(P)).then_inc(small_in, 16)
            act.wait_ge(consts_in, 16)
            for step in SCHEDULE:
                if step[0] == "front":
                    front(*step[1:])
                elif step[0] == "chunks":
                    for c in step[2]:
                        projection(("proj", step[1], c))
                elif step[0] == "collect":
                    projection(step[1])
                elif step[0] == "dots":
                    gelu(step[1])
                elif step[0] == "units":
                    s, a, b = step[1:]
                    a, b = UNITS * s + a, UNITS * s + b
                    if a == 0:
                        unit(0)
                        a = 1
                    if b - a > 1:
                        with act.Fori(a, b) as u:
                            unit(u)
                    elif b > a:
                        unit(a)
                elif step[0] == "close":
                    s = step[1]
                    for u in range(UNITS * (s + 1) - AHEAD, UNITS * (s + 1)):
                        unit(u, with_down=s < 3)
                    act.wait_ge(up_done, PH * TK * (s + 1))
                    for c in range(2):
                        nc.scalar.copy(x[:, STAGES[s][1], CW * c:CW * c + CW], acc[c][:, :]).then_inc(x_out_ready, 1)

        @block.tensor
        def _(pe):
            def transposes(kind, s, src):
                for i in range(2):
                    use = (kind, s, i)
                    tp.wait_room(pe, use)
                    for k in range(4):
                        last = nc.tensor.transpose(tp.bank(use)[:, k * P:(k + 1) * P],
                                                   src[:, (4 * i + k) * P:(4 * i + k + 1) * P], ident)
                    last.then_inc(tp_full, 1)

            def project(use, tiles=range(KT)):
                banks = banks_of(use)
                a, b = columns(use)
                chunk = ("wq", 0, 0) if use == REST else use
                tokens = h1_t[use[1]] if use[0] == "proj" else act_t
                if tiles[0] == 0:
                    pe.wait_ge(weights_in[place[chunk]], 16 * (same_place[chunk].index(chunk) + 1))
                    banks.wait_room(pe, use)
                    if use[0] == "proj":
                        for i in range(2):
                            tp.wait_evacuated(pe, ("h1", use[1], i))
                for k in tiles:
                    last = nc.tensor.matmul(banks.bank(use)[:, 0:b - a], tokens[:, k, :],
                                            chunk_at[place[chunk]][:, k, a:b],
                                            start=(k == 0), stop=(k == KT - 1))
                if k == KT - 1:
                    last.then_inc(banks.full, 1)

            def key_scores(s, g):
                use = ("sc", s, g)
                tp.wait_evacuated(pe, ("pq", s, g))
                mm.wait_room(pe, use)
                for i in range(4):
                    last = nc.tensor.matmul(mm.bank(use)[:, i * NK:(i + 1) * NK], q_t[0:HD, 4 * g + i, :],
                                            keys[:, 4 * g + i, :], start=True, stop=True)
                last.then_inc(mm_full, 1)

            def front(s, piece):
                l, t = STAGES[s]
                nkeys = (t + 1) * P
                if piece == "turn":
                    pe.wait_ge(h1_ready, s + 1)
                    transposes("h1", s, h_attn)
                elif piece in PIECE_CHUNKS:
                    for c in PIECE_CHUNKS[piece]:
                        project(("proj", s, c))
                elif piece == "decay":
                    use = ("F", s)
                    pe.wait_ge(log_f_ready, s + 1)
                    mm.wait_room(pe, use)
                    if t:
                        nc.tensor.matmul(mm.bank(use)[:, 0:8], ones, log_f[:, 0, :], start=True, stop=False)
                    nc.tensor.matmul(mm.bank(use)[:, 0:8], tri, log_f[:, t, :], start=(t == 0),
                                     stop=True).then_inc(mm_full, 1)
                elif piece == "heads":
                    pe.wait_ge(aug_ready, s + 1)
                    for g in range(8 if l == 0 else 5):
                        use = ("qk", s, g)
                        tp.wait_room(pe, use)
                        for i, (place, _, rows) in enumerate(qk_group(s, g)):
                            last = nc.tensor.transpose(tp.bank(use)[0:rows, i * P:(i + 1) * P], aug[:, place, 0:rows], ident)
                        last.then_inc(tp_full, 1)
                elif piece.startswith("attn"):
                    first, end = attn_heads(piece)
                    for g in range(8 if l == 0 else 5):
                        tp.wait_evacuated(pe, ("qk", s, g))

                    def scores(j):
                        use = ("S", s, j)
                        rows = k_rows(l, j)
                        mm.wait_room(pe, use)
                        kj = j if l == 0 else j // 8
                        nc.tensor.matmul(mm.bank(use)[:, 0:nkeys], q_t[0:rows, j, :], k_t[0:rows, kj, 0:nkeys],
                                         start=True, stop=True).then_inc(mm_full, 1)

                    def values(j):
                        use = ("PT", s, j)
                        tp.wait_evacuated(pe, use)
                        if j % 8 == 0 and s:
                            pe.wait_ge(o_free, 2 * (s - 1) + j // 8 + 1)
                        o = o_banks[j // 8][:, (j % 8) * HD:(j % 8 + 1) * HD]
                        for i in range(t + 1):
                            last = nc.tensor.matmul(o, probs_t[:, j % 2, i * P:(i + 1) * P], v[:, i, v_cols(l, j)],
                                                    start=(i == 0), stop=(i == t))
                        last.then_inc(pv_done, 1)

                    scores(first)
                    scores(first + 1)
                    for j in range(first, end):
                        use = ("PT", s, j)
                        tp.wait_room(pe, use)
                        pe.wait_ge(probs_ready, HEADS * s + j + 1)
                        for i in range(t + 1):
                            last = nc.tensor.transpose(tp.bank(use)[:, i * P:(i + 1) * P],
                                                       probs[:, j % 2, i * P:(i + 1) * P], ident)
                        last.then_inc(tp_full, 1)
                        if j + 2 < end:
                            scores(j + 2)
                        if j > first:
                            values(j - 1)
                        other, k = companion(s, j)
                        if other:
                            project(other, [k])
                    values(end - 1)
                elif piece == "out":
                    pe.wait_ge(o_free, 2 * s + 2)
                    if l == 0:
                        pe.wait_ge(gated, s + 1)
                    transposes("att", s, attended)
                    for i in range(2):
                        tp.wait_evacuated(pe, ("att", s, i))
                    for c in range(2):
                        project(("out", s, c))
                elif piece == "ffn":
                    pe.wait_ge(h2_ready, s + 1)
                    transposes("h2", s, h_ffn[:, s % 2, :])
                    for i in range(2):
                        tp.wait_evacuated(pe, ("h2", s, i))
                elif piece in ("wq0", "wq1"):
                    c = int(piece[2])
                    project(("wq", s, c))
                    mm.wait_evacuated(pe, ("wq", s, c))
                    for g in (2 * c, 2 * c + 1):
                        use = ("pq", s, g)
                        tp.wait_room(pe, use)
                        for i in range(4):
                            last = nc.tensor.transpose(tp.bank(use)[0:HD, i * P:(i + 1) * P],
                                                       queries[:, (4 * g + i) * HD:(4 * g + i + 1) * HD], ident)
                        last.then_inc(tp_full, 1)
                        if g == 0:
                            pe.wait_ge(keys_in, 16 * (l + 1))
                            key_scores(s, 0)
                            if s == 0:
                                project(REST)
                                side.wait_evacuated(pe, REST)
                elif next_scores(s, piece):
                    key_scores(s, next_scores(s, piece))

            def residual(s):
                wait_residual(pe, s)
                if s:
                    pe.wait_ge(x_out_ready, 2 * s)
                else:
                    for use in SIDE[-2:]:
                        side.wait_evacuated(pe, use)
                for c in range(2):
                    nc.tensor.matmul(acc[c][:, :], ident, x[:, STAGES[s][1], CW * c:CW * c + CW], start=True, stop=False,
                                     skip_group_check=True)

            def unit(u, last=False):
                for k in range(RING):
                    pe.wait_ge(diag_ready, RING * u + k + 1)
                    pe.wait_ge(up_in[k], 16 * (u + 1))
                    for c in range(2):
                        ins = nc.tensor.matmul(acc[c][:, :], diags[:, k, :], up_rows[:, k, CW * c:CW * c + CW],
                                               start=False, stop=(last and k == RING - 1), skip_group_check=True)
                    ins.then_inc(up_done, 1)

            pe.wait_ge(consts_in, 16)
            for step in SCHEDULE:
                if step[0] == "front":
                    front(*step[1:])
                elif step[0] == "chunks":
                    for c in step[2]:
                        project(("proj", step[1], c))
                elif step[0] == "multiply":
                    project(step[1])
                elif step[0] == "open":
                    if step[1] == 0:
                        key_scores(0, 1)
                    residual(step[1])
                elif step[0] == "units":
                    s, a, b = step[1:]
                    a, b = UNITS * s + a, UNITS * s + b
                    if b > a + 1:
                        with pe.Fori(a, b) as u:
                            unit(u)
                    else:
                        unit(a)
                elif step[0] == "close":
                    s = step[1]
                    for u in range(UNITS * (s + 1) - AHEAD, UNITS * (s + 1)):
                        unit(u, last=u == UNITS * (s + 1) - 1)

        @block.vector
        def _(dve):
            steps = [0]

            def tick(ins):
                steps[0] += 1
                return ins.then_inc(dve_step, 1)

            def settle():
                dve.wait_ge(dve_step, steps[0])

            def link(ins):
                tick(ins)
                settle()

            def norm(x_t, gain, dst):
                link(nc.vector.reciprocal(rstd[:, :], rms[:, :]))
                return nc.vector.scalar_tensor_tensor(dst, x_t, rstd[:, 0:1], gain[:, :], ALU.mult, ALU.mult)

            def top16(values, place_v, place_i, scratch):
                link(nc.vector.max(place_v[:, 0:8], values))
                tick(nc.vector.max_index(place_i[:, 0:8], place_v[:, 0:8], values))
                link(nc.vector.match_replace(scratch, place_v[:, 0:8], values, -BIG))
                link(nc.vector.max(place_v[:, 8:16], scratch))
                return nc.vector.max_index(place_i[:, 8:16], place_v[:, 8:16], scratch)

            def projection(use):
                _, s, c = use
                l = STAGES[s][0]
                if head_span(l, c):
                    a, n, gain = head_span(l, c)
                    dve.wait_ge(squares_ready, norm_no[use] + 1)
                    nc.vector.tensor_reduce(head_ss[:, 0:n], squares[:, 0:n, :], AX_X, ALU.add).then_inc(head_ss_ready, 1)
                    dve.wait_ge(head_rms_ready, norm_no[use] + 1)
                    link(nc.vector.reciprocal(head_ss[:, 0:n], head_ss[:, 0:n]))
                    heads = aug[:, a:a + n, 0:HD]
                    link(nc.vector.tensor_tensor(heads, heads, head_ss[:, 0:n].unsqueeze(2).to_broadcast([P, n, HD]), ALU.mult))
                    link(nc.vector.tensor_tensor(heads, heads, g_heads[l][:, gain:gain + 1, :].to_broadcast([P, n, HD]), ALU.mult))
                if (l, c) != (0, 7):
                    return
                mm.wait_full(dve, use)
                nc.vector.tensor_tensor(fz[:, STAGES[s][1], 0, :], mm.bank(use)[:, 0:8], f_bias[:, :],
                                        ALU.add).then_inc(mm.freed(use), 1)
                mm.wait_evacuated(dve, use)

            def front(s, piece):
                l, t = STAGES[s]
                nkeys = (t + 1) * P
                if piece == "norm":
                    dve.wait_ge(rms1_ready, s + 1)
                    dve.wait_ge(attn_gain_in, 16 * (l + 1))
                    norm(x[:, t, :], gain_attn, h_attn).then_inc(h1_ready, 1)
                    if s == 0:
                        dve.wait_ge(small_in, 4 * 16)
                        for g in (g_heads[0][:, 0, :], g_heads[0][:, 2, :], g_heads[1][:, 0, :]):
                            link(nc.vector.tensor_scalar(g, g, SCALE, None, ALU.mult))
                        link(nc.vector.tensor_scalar(neg_sink[:, :], sink[:, :], -1.0, None, ALU.mult))
                elif piece in PIECE_CHUNKS:
                    for c in PIECE_CHUNKS[piece]:
                        projection(("proj", s, c))
                elif piece == "forget":
                    z, neg, low = fz[:, t, 0, :], fz[:, t, 1, :], fz[:, t, 0, :]
                    link(nc.vector.tensor_scalar(neg, z, -1.0, None, ALU.mult))
                    nc.vector.tensor_tensor(neg, z, neg, ALU.min).then_inc(fz_ready, 1)
                    link(nc.vector.tensor_scalar(low, z, 0.0, None, ALU.min))
                    dve.wait_ge(fln_ready, s + 1)
                    nc.vector.tensor_tensor(log_f[:, t, :], low, fz[:, t, 3, :], ALU.subtract).then_inc(log_f_ready, 1)
                elif piece == "decay":
                    use = ("F", s)
                    mm.wait_full(dve, use)
                    f = mm.bank(use)[:, 0:8].unsqueeze(2)
                    nc.vector.tensor_copy(aug[:, 16:24, HD:HD + 1], f)
                    nc.vector.tensor_scalar(aug[:, 24:32, HD + 1:HD + 2], f, -1.0, None, ALU.mult).then_inc(mm.freed(use), 1)
                    nc.vector.memset(aug[:, 16:24, HD + 1:HD + 2], 1.0)
                    nc.vector.memset(aug[:, 24:32, HD:HD + 1], 1.0)
                elif piece == "heads":
                    n = 16 if l == 0 else 18
                    cos = cst[:, C_COS + ROT * t:C_COS + ROT * (t + 1)].unsqueeze(1).to_broadcast([P, n, ROT])
                    sin = cst[:, C_SIN + ROT * t:C_SIN + ROT * (t + 1)].unsqueeze(1).to_broadcast([P, n, ROT])
                    x1, x2 = aug[:, 0:n, 0:ROT], aug[:, 0:n, ROT:2 * ROT]
                    for i, (a, b) in enumerate(((x1, cos), (x2, sin), (x2, cos), (x1, sin))):
                        tick(nc.vector.tensor_tensor(rope_tmp[:, i, 0:n, :], a, b, ALU.mult))
                    settle()
                    nc.vector.tensor_tensor(x1, rope_tmp[:, 0, 0:n, :], rope_tmp[:, 1, 0:n, :], ALU.subtract)
                    nc.vector.tensor_tensor(x2, rope_tmp[:, 2, 0:n, :], rope_tmp[:, 3, 0:n, :],
                                            ALU.add).then_inc(aug_ready, 1)
                elif piece == "gate":
                    banks_of(("proj", s, 6)).wait_evacuated(dve, ("proj", s, 6))
                    link(nc.vector.tensor_scalar(gate[:, t, :], gate[:, t, :], 1.0, None, ALU.add))
                    link(nc.vector.reciprocal(gate[:, t, :], gate[:, t, :]))
                elif piece.startswith("attn"):
                    first, end = attn_heads(piece)
                    mask = masks[l][:, 2 * P - nkeys:2 * P]
                    for j in range(first, end):
                        use = ("S", s, j)
                        mm.wait_full(dve, use)
                        if j >= 2:
                            tp.wait_full(dve, ("PT", s, j - 2))
                        nc.vector.tensor_tensor_reduce(
                            out=probs[:, j % 2, 0:nkeys], in0=mm.bank(use)[:, 0:nkeys], in1=mask, scale=-1.0,
                            scalar=neg_sink[:, j:j + 1] if l == 1 else BIG, op0=ALU.add, op1=ALU.min,
                            accum_out=neg_max[:, j:j + 1]).then_inc(mm.freed(use), 1)
                        if j % 8 == 7:
                            i = j // 8
                            heads = slice(8 * i, 8 * i + 8)
                            if l == 1:
                                for i2 in (j - 1, j):
                                    mm.wait_evacuated(dve, ("S", s, i2))
                                nc.vector.tensor_tensor(sink_e[:, heads], sink[:, heads], neg_max[:, heads],
                                                        ALU.add).then_inc(sink_in_ready, 1)
                                dve.wait_ge(sink_e_ready, 2 * t + i + 1)
                                dve.wait_ge(probs_ready, HEADS * s + j + 1)
                                link(nc.vector.tensor_tensor(row_sum[:, heads], row_sum[:, heads], sink_e[:, heads], ALU.add))
                            dve.wait_ge(probs_ready, HEADS * s + j + 1)
                            link(nc.vector.reciprocal(row_sum[:, heads], row_sum[:, heads]))
                elif piece == "out":
                    for i in range(2):
                        dve.wait_ge(pv_done, HEADS * s + 8 * (i + 1))
                        heads = slice(8 * i, 8 * i + 8)
                        o = attended[:, CW * i:CW * i + CW].rearrange("p (h d) -> p h d", d=HD)
                        ins = nc.vector.tensor_tensor(
                            o, o_banks[i][:, :].rearrange("p (h d) -> p h d", d=HD),
                            row_sum[:, heads].unsqueeze(2).to_broadcast([P, 8, HD]), ALU.mult)
                        ins.then_inc(o_free, 1)
                    if l == 0:
                        dve.wait_ge(o_free, 2 * s + 2)
                        nc.vector.tensor_tensor(attended[:, CW:2 * CW], attended[:, CW:2 * CW], gate[:, t, :],
                                                ALU.mult).then_inc(gated, 1)
                    for c in range(2):
                        use = ("out", s, c)
                        mm.wait_full(dve, use)
                        xc = x[:, t, CW * c:CW * c + CW]
                        nc.vector.tensor_tensor(xc, xc, mm.bank(use)[:, :], ALU.add).then_inc(mm.freed(use), 1)
                elif piece == "ffn":
                    dve.wait_ge(rms2_ready, s + 1)
                    dve.wait_ge(norms_in, 16 * (l + 1))
                    norm(x[:, t, :], gain_ffn, h_ffn[:, s % 2, :]).then_inc(h2_ready, 1)
                elif piece.startswith("topk"):
                    h = int(piece[4])
                    use = ("sc", s, h // 2)
                    mm.wait_full(dve, use)
                    for i in range(2):
                        first = (2 * (h % 2) + i) * NK
                        last = top16(mm.bank(use)[:, first:first + NK], top_v[:, i, :], top_i[:, i, :], rest[:, 0:NK])
                        if h % 2 and i:
                            last.then_inc(mm.freed(use), 1)
                            mm.wait_evacuated(dve, use)
                        else:
                            tick(last)
                    settle()
                    tick(nc.vector.tensor_copy(top_if[:, :, :], top_i[:, :, :]))
                    link(nc.vector.tensor_tensor(
                        cand[:, :].rearrange("p (a b) -> p a b", a=TK),
                        top_v[:, 0, :].unsqueeze(2).to_broadcast([P, TK, TK]),
                        top_v[:, 1, :].unsqueeze(1).to_broadcast([P, TK, TK]), ALU.add))
                    link(top16(cand[:, :], best_v[:, h % 2, :], best_i[:, :], rest[:, :]))
                    nc.vector.tensor_scalar(neg_best[:, h % 2:h % 2 + 1], best_v[:, h % 2, 0:1], -1.0, None, ALU.mult).then_inc(best_ready, 1)
                    tick(nc.vector.tensor_single_scalar(half_i[:, 0, :], best_i[:, :], 4, ALU.logical_shift_right))
                    link(nc.vector.tensor_single_scalar(half_i[:, 1, :], best_i[:, :], 15, ALU.bitwise_and))
                    link(nc.vector.tensor_copy(half_f[:, :, :], half_i[:, :, :]))
                    flat = onehot.rearrange("p h a b -> p (h a) b")
                    link(nc.vector.tensor_tensor(
                        flat, half_f[:, :, :].rearrange("p h a -> p (h a)").unsqueeze(2).to_broadcast([P, 2 * TK, TK]),
                        iota.unsqueeze(1).to_broadcast([P, 2 * TK, TK]), ALU.is_equal))
                    link(nc.vector.tensor_tensor(
                        onehot, onehot, top_if[:, :, :].unsqueeze(2).to_broadcast([P, 2, TK, TK]), ALU.mult))
                    link(nc.vector.tensor_reduce(chosen[:, :, :].rearrange("p h a -> p (h a)"), flat, AX_X, ALU.add))
                    link(nc.vector.tensor_scalar(id_f[:, :], chosen[:, 0, :], float(NK), float(l * EXPERTS), ALU.mult, ALU.add))
                    link(nc.vector.tensor_tensor(id_f[:, :], id_f[:, :], chosen[:, 1, :], ALU.add))
                    at = TK * (PH * s + h)
                    nc.vector.tensor_copy(ids[:, at:at + TK], id_f[:, :]).then_inc(ids_ready, 1)
                elif piece.startswith("gates"):
                    h = int(piece[5])
                    at = TK * (PH * s + h)
                    total = g_sum[:, h % 2:h % 2 + 1]
                    dve.wait_ge(gexp_ready, PH * s + h + 1)
                    link(nc.vector.reciprocal(total, total))
                    link(nc.vector.tensor_scalar(gates[:, at:at + TK], best_v[:, h % 2, :], total, None, ALU.mult))

            def unit(u, s):
                for k in range(RING):
                    dve.wait_ge(down_in[k], 16 * (u + 1))
                    nc.vector.scalar_tensor_tensor(
                        down_rows[:, k, :], down_rows[:, k, :], 1.0, h_ffn[:, s % 2, :], ALU.mult, ALU.mult,
                        accum_out=dots[:, k:k + 1]).then_inc(dots_done, 1)
                dve.wait_ge(gelu_done, u + 1)
                now = gates[:, bass.ds(RING * u, RING)]
                nc.vector.tensor_tensor(now, gelus[:, :], now, ALU.mult).then_inc(w_ready, 1)

            dve.wait_ge(consts_in, 16)
            for step in SCHEDULE:
                if step[0] == "front":
                    front(*step[1:])
                elif step[0] == "chunks":
                    for c in step[2]:
                        projection(("proj", step[1], c))
                elif step[0] == "dots":
                    unit(step[1], 0)
                elif step[0] == "units":
                    s, a, b = step[1:]
                    a, b = UNITS * s + a + AHEAD, UNITS * s + b + AHEAD
                    if b - a > 1:
                        with dve.Fori(a, b) as u:
                            unit(u, s)
                    else:
                        unit(a, s)
                elif step[0] == "close" and step[1] < 3:
                    for u in range(AHEAD):
                        unit(UNITS * (step[1] + 1) + u, step[1] + 1)


def kernel(x, attn_norm, ffn_norm, ev_w_in, ev_forget_bias, ev_q_norm_a, ev_k_norm_a,
           ev_q_norm_b, ev_k_norm_b, ev_w_out, od_w_in, od_q_norm, od_k_norm, od_sinks,
           od_w_out, peer_w_query, peer_sub_keys, peer_down, peer_up):
    import numpy as np
    import concourse.bacc as bacc
    from concourse.bass_utils import run_bass_kernel_spmd

    seq = np.arange(2 * P, dtype=np.float32)
    inv_freq = np.power(np.float32(500000.0), -np.arange(0, 2 * ROT, 2, dtype=np.float32) / np.float32(2 * ROT))
    ang = (seq[:, None] * inv_freq[None, :]).astype(np.float32)
    c = np.zeros((P, C_END), np.float32)
    i, j = np.arange(P)[:, None], np.arange(P)[None, :]
    c[:, C_ID:C_ID + P] = i == j
    c[:, C_M0 + P:C_M0 + 2 * P] = np.where(j <= i, 0.0, NEG_INF)
    c[:, C_M1 + P:C_M1 + 2 * P] = np.where(j <= i, 0.0, NEG_INF)
    c[:, C_M1:C_M1 + P] = np.where(j > i, 0.0, NEG_INF)
    c[:, C_TRI:C_TRI + P] = i <= j
    c[:, C_ONES:C_ONES + P] = 1.0
    for t in range(2):
        c[:, C_COS + ROT * t:C_COS + ROT * (t + 1)] = np.cos(ang[P * t:P * (t + 1)])
        c[:, C_SIN + ROT * t:C_SIN + ROT * (t + 1)] = np.sin(ang[P * t:P * (t + 1)])
    c[:, C_IOTA:C_IOTA + TK] = np.arange(TK)
    c[:, C_EPS] = EPS
    con = np.ascontiguousarray
    a = np.asarray
    arrays = {
        "x_in": con(a(x)[0]), "consts": c, "attn_norm": con(a(attn_norm)), "ffn_norm": con(a(ffn_norm)),
        "w_in0": con(a(ev_w_in)[0]), "fbias": con(a(ev_forget_bias)[0]),
        "head_gains0": np.stack([a(ev_q_norm_a)[0], a(ev_k_norm_a)[0], a(ev_q_norm_b)[0], a(ev_k_norm_b)[0]]),
        "w_out0": con(a(ev_w_out)[0]), "w_in1": con(a(od_w_in)[0]),
        "head_gains1": np.stack([a(od_q_norm)[0], a(od_k_norm)[0]]), "sinks": con(a(od_sinks)[0]),
        "w_out1": con(a(od_w_out)[0]), "w_query": con(a(peer_w_query)),
        "keys_t": con(a(peer_sub_keys).transpose(4, 0, 1, 2, 3).reshape(HD, 2, 2 * PH, NK)),
        "down": con(a(peer_down).reshape(2 * EXPERTS, D)), "up": con(a(peer_up).reshape(2 * EXPERTS, D)),
    }
    nc = bacc.Bacc("TRN2", target_bir_lowering=False, num_devices=1)
    args = [nc.dram_tensor(k, v.shape, mybir.dt.from_np(v.dtype), kind="ExternalInput").ap() for k, v in arrays.items()]
    args.append(nc.dram_tensor("out", (2 * P, D), F32, kind="ExternalOutput").ap())
    build(nc, *args)
    r = run_bass_kernel_spmd(nc, [arrays], core_ids=[0])
    return r.results[0]["out"].reshape(1, 2 * P, D)
```
